# Optimizing a Trainium2 kernel written in Bass

```python
import math
import jax
import jax.numpy as jnp
from jax import lax
import numpy as np

D_MODEL = 1024
BATCH = 1
SEQ = 1024
DEPTH = 2
DEC_BATCH = 1
DEC_SEQ = 32
PAST_LEN = 512

CHUNK = 64
ROPE_THETA = 10000.0
EPS = 1e-6
NEG_BIG = -1e30
LB_FLOOR = 1e-20
H_A = 6
DA = 32
DV_A = 64
H_B = 5
D_B = 64
H_I = 4
D_I = 64
TOPK_MAX = 256
H_C = 5
DK_C = 64
DV_C = 64
MIX = H_A * DV_A + H_B * D_B + H_C * DV_C
D_FF = 2816
CONV_W = 3
QB_A = 128
QB_B = CHUNK
IN_SIZES = (H_A * 2 * DA, H_A * 2 * DA, H_A * DV_A,
            H_B * D_B, H_B * D_B, H_B * D_B,
            H_I * D_I, D_I, H_I,
            H_C * DK_C, H_C * DK_C, H_C * DV_C, H_C * DV_C)
W_IN = int(sum(IN_SIZES))
IN_OFFSETS = tuple(int(o) for o in np.cumsum(IN_SIZES)[:-1])

kernel_name = "hymba_style_diff_dsa_hgrn2_streaming_step"

F32 = jnp.float32

def rmsnorm(x, gain):
    x32 = x.astype(F32)
    y = x32 * lax.rsqrt(jnp.mean(x32 * x32, axis=-1, keepdims=True) + EPS)
    return (y * gain.astype(F32)).astype(x.dtype)

def rope_tables(pos, dim):
    inv_freq = ROPE_THETA ** (-jnp.arange(0, dim, 2, dtype=F32) / dim)
    ang = pos.astype(F32)[:, None] * inv_freq[None, :]
    return jnp.cos(ang), jnp.sin(ang)

def apply_rope(x, cos, sin):
    shape = (1, cos.shape[0]) + (1,) * (x.ndim - 3) + (cos.shape[1],)
    c = cos.reshape(shape)
    s = sin.reshape(shape)
    x1, x2 = jnp.split(x.astype(F32), 2, axis=-1)
    return jnp.concatenate([x1 * c - x2 * s, x2 * c + x1 * s], axis=-1).astype(x.dtype)

def to_blocks(x, qb):
    b, t = x.shape[:2]
    return jnp.moveaxis(x.reshape((b, t // qb, qb) + x.shape[2:]), 1, 0)

def from_blocks(y):
    y = jnp.moveaxis(y, 0, 1)
    return y.reshape((y.shape[0], y.shape[1] * y.shape[2]) + y.shape[3:])

def mixer_inputs(xn, w, pos, lb):
    b, t, _ = xn.shape
    u = xn @ w
    aq, ak, av, bq, bk, bv, iq, ik, iw, cq, cf, ci, cg = jnp.split(u, IN_OFFSETS, axis=-1)
    cos_a, sin_a = rope_tables(pos, DA)
    cos_b, sin_b = rope_tables(pos, D_B)
    cos_i, sin_i = rope_tables(pos, D_I)
    aq = apply_rope(aq.reshape(b, t, H_A, 2, DA), cos_a, sin_a)
    ak = apply_rope(ak.reshape(b, t, H_A, 2, DA), cos_a, sin_a)
    av = av.reshape(b, t, H_A, DV_A)
    bq = apply_rope(bq.reshape(b, t, H_B, D_B), cos_b, sin_b)
    bk = apply_rope(bk.reshape(b, t, H_B, D_B), cos_b, sin_b)
    bv = bv.reshape(b, t, H_B, D_B)
    iq = apply_rope(iq.reshape(b, t, H_I, D_I), cos_i, sin_i)
    ik = apply_rope(ik, cos_i, sin_i)
    iw = iw * (H_I ** -0.5)
    z = cf.astype(F32).reshape(b, t, H_C, DK_C)
    lbh = lb.reshape(H_C, DK_C)
    cgl = jnp.logaddexp(jnp.log(jnp.maximum(lbh, LB_FLOOR)), jnp.log1p(-lbh) + jax.nn.log_sigmoid(z))
    ck = (1.0 - lbh) * jax.nn.sigmoid(-z)
    cqf = jax.nn.silu(cq.astype(F32)).reshape(b, t, H_C, DK_C)
    cv = ci.astype(F32).reshape(b, t, H_C, DV_C)
    cgate = cg.reshape(b, t, H_C, DV_C)
    return aq, ak, av, bq, bk, bv, iq, ik, iw, cqf, ck, cgl, cv, cgate

def diff_attend(q, k, v, mask, lam):
    s = jnp.einsum('bqhmd,bkhmd->bhmqk', q, k, preferred_element_type=F32) * (DA ** -0.5)
    if mask is not None:
        s = jnp.where(mask, s, NEG_BIG)
    p = jax.nn.softmax(s, axis=-1)
    a = p[:, :, 0] - lam * p[:, :, 1]
    return jnp.einsum('bhqk,bkhd->bqhd', a.astype(v.dtype), v)

def diff_attn_prompt(q, k, v, lam):
    t = q.shape[1]
    kchunk = jnp.arange(t) // CHUNK

    def blk(args):
        qb, i = args
        qchunk = (i * QB_A + jnp.arange(QB_A)) // CHUNK
        mask = kchunk[None, :] <= qchunk[:, None]
        return diff_attend(qb, k, v, mask, lam)

    out = lax.map(blk, (to_blocks(q, QB_A), jnp.arange(t // QB_A)))
    return from_blocks(out)

def dsa_attend(q, qi, wi, k_all, v_all, ki_all, mask, n_sel):
    dots = jnp.einsum('bqhd,bsd->bqhs', qi, ki_all, preferred_element_type=F32) * (D_I ** -0.5)
    score = jnp.einsum('bqh,bqhs->bqs', wi.astype(F32), jax.nn.relu(dots))
    if mask is not None:
        score = jnp.where(mask, score, NEG_BIG)
    _, sel = lax.top_k(score, n_sel)
    gather = jax.vmap(lambda a, i: a[i])
    k_sel = gather(k_all, sel)
    v_sel = gather(v_all, sel)
    s = jnp.einsum('bqhd,bqkhd->bhqk', q, k_sel, preferred_element_type=F32) * (D_B ** -0.5)
    if mask is not None:
        valid = mask[jnp.arange(q.shape[1])[None, :, None], sel]
        s = jnp.where(valid[:, None], s, NEG_BIG)
    p = jax.nn.softmax(s, axis=-1)
    return jnp.einsum('bhqk,bqkhd->bqhd', p.astype(v_sel.dtype), v_sel)

def dsa_prompt(q, qi, wi, k, v, ki):
    t = q.shape[1]
    n_sel = min(TOPK_MAX, t // 4)
    kchunk = jnp.arange(t) // CHUNK

    def blk(args):
        qb, qib, wib, i = args
        qchunk = (i * QB_B + jnp.arange(QB_B)) // CHUNK
        mask = kchunk[None, :] <= qchunk[:, None]
        return dsa_attend(qb, qib, wib, k, v, ki, mask, n_sel)

    out = lax.map(blk, (to_blocks(q, QB_B), to_blocks(qi, QB_B), to_blocks(wi, QB_B),
                        jnp.arange(t // QB_B)))
    return from_blocks(out)

def hgrn2_chunk(S, q, k, g, v):
    c = q.shape[1]
    bcum = jnp.cumsum(g, axis=1)
    causal = jnp.tril(jnp.ones((c, c), dtype=bool))[None, :, :, None, None]
    diff = bcum[:, :, None] - bcum[:, None, :]
    decay = jnp.where(causal, jnp.exp(jnp.where(causal, diff, 0.0)), 0.0)
    att = jnp.einsum('bthk,btshk,bshk->bhts', q, decay, k)
    o = (jnp.einsum('bhts,bshv->bthv', att, v)
         + jnp.einsum('bthk,bhkv->bthv', q * jnp.exp(bcum), S))
    b_last = bcum[:, -1]
    S_new = (jnp.exp(b_last)[..., None] * S
             + jnp.einsum('bshk,bshv->bhkv', k * jnp.exp(b_last[:, None] - bcum), v))
    return S_new, o

def hgrn2_prompt(q, k, g, v):
    b = q.shape[0]
    S0 = jnp.zeros((b, H_C, DK_C, DV_C), F32)
    xs = (to_blocks(q, CHUNK), to_blocks(k, CHUNK), to_blocks(g, CHUNK), to_blocks(v, CHUNK))
    S, o = lax.scan(lambda S, a: hgrn2_chunk(S, *a), S0, xs)
    return S, from_blocks(o)

def merge_heads(oa, ob, oc, cgate, lam_init, a_gain, c_gain, w_out):
    b, t = oa.shape[:2]
    oa = rmsnorm(oa, a_gain) * (1.0 - lam_init)
    oc = rmsnorm(oc, c_gain) * jax.nn.silu(cgate)
    cat = jnp.concatenate([oa.reshape(b, t, -1), ob.reshape(b, t, -1), oc.reshape(b, t, -1)], axis=-1)
    return cat @ w_out

def conv_ffn(h, hist, w_up, w_conv, b_conv, w_down):
    a, gate = jnp.split(h @ w_up, 2, axis=-1)
    t = a.shape[1]
    ext = jnp.concatenate([hist.astype(a.dtype), a], axis=1)
    conv = b_conv
    for j in range(CONV_W):
        conv = conv + ext[:, j:j + t] * w_conv[j]
    return (jax.nn.silu(conv) * gate) @ w_down, ext[:, t:]

def setup_inputs(seed: int = 0) -> dict:
    key = jax.random.key(seed)
    ks = jax.random.split(key, 25)

    def nrm(k, shape, scale):
        return scale * jax.random.normal(k, shape, F32)

    return {
        "x_prompt": nrm(ks[0], (BATCH, SEQ, D_MODEL), 1.0),
        "x_sample": nrm(ks[1], (DEC_BATCH, DEC_SEQ, D_MODEL), 1.0),
        "cache_a_k": nrm(ks[2], (DEPTH, DEC_BATCH, PAST_LEN, H_A, 2 * DA), 1.0),
        "cache_a_v": nrm(ks[3], (DEPTH, DEC_BATCH, PAST_LEN, H_A, DV_A), 1.0),
        "cache_b_k": nrm(ks[4], (DEPTH, DEC_BATCH, PAST_LEN, H_B, D_B), 1.0),
        "cache_b_v": nrm(ks[5], (DEPTH, DEC_BATCH, PAST_LEN, H_B, D_B), 1.0),
        "cache_b_kidx": nrm(ks[6], (DEPTH, DEC_BATCH, PAST_LEN, D_I), 1.0),
        "state_c": nrm(ks[7], (DEPTH, DEC_BATCH, H_C, DK_C, DV_C), 0.3),
        "state_ffn_conv": nrm(ks[8], (DEPTH, DEC_BATCH, CONV_W - 1, D_FF), 1.0),
        "norm1": 1.0 + nrm(ks[9], (DEPTH, D_MODEL), 0.02),
        "w_in": nrm(ks[10], (DEPTH, D_MODEL, W_IN), D_MODEL ** -0.5),
        "lam_q1": nrm(ks[11], (DEPTH, DA), 0.1),
        "lam_k1": nrm(ks[12], (DEPTH, DA), 0.1),
        "lam_q2": nrm(ks[13], (DEPTH, DA), 0.1),
        "lam_k2": nrm(ks[14], (DEPTH, DA), 0.1),
        "a_norm": 1.0 + nrm(ks[15], (DEPTH, DV_A), 0.02),
        "c_lower": nrm(ks[16], (DEPTH, H_C * DK_C), 0.1),
        "c_norm": 1.0 + nrm(ks[17], (DEPTH, DV_C), 0.02),
        "w_out": nrm(ks[18], (DEPTH, MIX, D_MODEL), 0.5 * MIX ** -0.5),
        "norm2": 1.0 + nrm(ks[19], (DEPTH, D_MODEL), 0.02),
        "ffn_up": nrm(ks[20], (DEPTH, D_MODEL, 2 * D_FF), D_MODEL ** -0.5),
        "ffn_conv_w": nrm(ks[21], (DEPTH, CONV_W, D_FF), CONV_W ** -0.5),
        "ffn_conv_b": nrm(ks[22], (DEPTH, D_FF), 0.01),
        "ffn_down": nrm(ks[23], (DEPTH, D_FF, D_MODEL), 0.5 * D_FF ** -0.5),
        "final_norm": 1.0 + nrm(ks[24], (D_MODEL,), 0.02),
    }

def reference(x_prompt, x_sample, cache_a_k, cache_a_v, cache_b_k, cache_b_v, cache_b_kidx, state_c,
              state_ffn_conv, norm1, w_in, lam_q1, lam_k1, lam_q2, lam_k2, a_norm, c_lower, c_norm, w_out,
              norm2, ffn_up, ffn_conv_w, ffn_conv_b, ffn_down, final_norm):
    t_p = x_prompt.shape[1]
    past = cache_a_k.shape[2]
    t_s = x_sample.shape[1]
    pos_p = jnp.arange(t_p)
    pos_s = past + jnp.arange(t_s)
    n_sel_s = min(TOPK_MAX, (past + t_s) // 4)
    lb_soft = jax.nn.softmax(c_lower.astype(F32), axis=0)
    lower = jnp.cumsum(lb_soft, axis=0) - lb_soft[0]

    xp, xs = x_prompt, x_sample
    akp, avp, bkp, bvp, bip, scp, fcp = [], [], [], [], [], [], []
    aks, avs, bks, bvs, bis, scs, fcs = [], [], [], [], [], [], []
    for l in range(DEPTH):
        lam_init = 0.8 - 0.6 * math.exp(-0.3 * l)
        lam = (jnp.exp(jnp.sum(lam_q1[l].astype(F32) * lam_k1[l].astype(F32)))
               - jnp.exp(jnp.sum(lam_q2[l].astype(F32) * lam_k2[l].astype(F32))) + lam_init)

        aq, ak, av, bq, bk, bv, iq, ik, iw, cq, ck, cg, cv, cgate = mixer_inputs(
            rmsnorm(xp, norm1[l]), w_in[l], pos_p, lower[l])
        oa = diff_attn_prompt(aq, ak, av, lam)
        ob = dsa_prompt(bq, iq, iw, bk, bv, ik)
        sc, oc = hgrn2_prompt(cq, ck, cg, cv)
        xp = xp + merge_heads(oa, ob, oc.astype(xp.dtype), cgate, lam_init, a_norm[l], c_norm[l], w_out[l])
        hist0 = jnp.zeros((xp.shape[0], CONV_W - 1, D_FF), xp.dtype)
        h, fc = conv_ffn(rmsnorm(xp, norm2[l]), hist0, ffn_up[l], ffn_conv_w[l], ffn_conv_b[l], ffn_down[l])
        xp = xp + h
        b_p = xp.shape[0]
        akp.append(ak.reshape(b_p, t_p, H_A, 2 * DA))
        avp.append(av)
        bkp.append(bk)
        bvp.append(bv)
        bip.append(ik)
        scp.append(sc.astype(xp.dtype))
        fcp.append(fc)

        aq, ak, av, bq, bk, bv, iq, ik, iw, cq, ck, cg, cv, cgate = mixer_inputs(
            rmsnorm(xs, norm1[l]), w_in[l], pos_s, lower[l])
        b_s = xs.shape[0]
        ka = jnp.concatenate([cache_a_k[l].reshape(b_s, past, H_A, 2, DA).astype(ak.dtype), ak], axis=1)
        va = jnp.concatenate([cache_a_v[l].astype(av.dtype), av], axis=1)
        oa = diff_attend(aq, ka, va, None, lam)
        kb = jnp.concatenate([cache_b_k[l].astype(bk.dtype), bk], axis=1)
        vb = jnp.concatenate([cache_b_v[l].astype(bv.dtype), bv], axis=1)
        kib = jnp.concatenate([cache_b_kidx[l].astype(ik.dtype), ik], axis=1)
        ob = dsa_attend(bq, iq, iw, kb, vb, kib, None, n_sel_s)
        sc, oc = hgrn2_chunk(state_c[l].astype(F32), cq, ck, cg, cv)
        xs = xs + merge_heads(oa, ob, oc.astype(xs.dtype), cgate, lam_init, a_norm[l], c_norm[l], w_out[l])
        h, fc = conv_ffn(rmsnorm(xs, norm2[l]), state_ffn_conv[l], ffn_up[l], ffn_conv_w[l], ffn_conv_b[l],
                         ffn_down[l])
        xs = xs + h
        aks.append(ak.reshape(b_s, t_s, H_A, 2 * DA))
        avs.append(av)
        bks.append(bk)
        bvs.append(bv)
        bis.append(ik)
        scs.append(sc.astype(state_c.dtype))
        fcs.append(fc)

    y_prompt = rmsnorm(xp, final_norm)
    y_sample = rmsnorm(xs, final_norm)
    return (y_prompt, y_sample,
            jnp.stack(akp), jnp.stack(avp), jnp.stack(bkp), jnp.stack(bvp), jnp.stack(bip),
            jnp.stack(scp), jnp.stack(fcp),
            jnp.stack(aks), jnp.stack(avs), jnp.stack(bks), jnp.stack(bvs), jnp.stack(bis),
            jnp.stack(scs), jnp.stack(fcs))


_drawn_inputs = setup_inputs


def setup_inputs(seed=0):
    import zlib

    import numpy as np

    out = dict(_drawn_inputs(seed))
    spreads = {}
    factors = {'state_c': 3.891,
     'lam_q2': 3.852,
     'lam_k2': 5.946,
     'a_norm': 7.896,
     'c_norm': 24.656,
     'norm2': 2.79,
     'ffn_conv_b': 8.0,
     'final_norm': 8.109,
     'cache_b_k': 2.905}
    for name, (base, spread) in spreads.items():
        noise = np.random.default_rng([zlib.crc32(name.encode()), seed]).standard_normal(out[name].shape)
        drawn = base * np.exp(spread * noise) if base else spread * noise
        out[name] = jnp.asarray(drawn.astype(out[name].dtype))
    for name, factor in factors.items():
        out[name] = (out[name] * factor).astype(out[name].dtype)
    return out
```

```python
import concourse.bass as bass
from concourse import mybir
from contextlib import ExitStack

F32 = mybir.dt.float32
ALU = mybir.AluOpType
ACT = mybir.ActivationFunctionType
AX = mybir.AxisListType.X

P = 128
L, DM, TP, TS, PAST = 2, 1024, 1024, 32, 512
T = TP + TS
NJ, JW = 3, 352
KD = DM // P
HA, HB, HC, HI, D = 6, 5, 5, 4, 64
DFF = 2816
NF = DFF // P
NT = TP // P
EPS = 1e-6
NEG = -1e30
SENTINEL = -3e38
TOP_P, TOP_S = 256, (PAST + TS) // 4
R_AQ, R_AK, R_IQ, R_IK, R_BQ, R_BK, R_CQ, R_CF = 0, 384, 768, 1024, 1088, 1408, 1728, 2048
NPT = 19
C_AV, C_BV, C_IW, C_CI, C_CG, WN = 0, 384, 704, 708, 1028, 1348
NC4, CW = 4, WN // 4
P_N1, P_N2, P_CONV, P_HIST, P_AG, P_CG, P_LAM, P_LI, PCOLS = 0, 8, 16, 104, 148, 212, 276, 404, 406
UNITS = [(i * P, P, (i + 1) * P) for i in range(NT)] + [(TP, TS, PAST + TS)]
NU = len(UNITS)
KEY0 = [0] * NT + [TP]
VT0 = [0] * NT + [NT]
GROUPS = [[list(range(a, min(a + 4, -(-nk // P)))) for a in range(0, -(-nk // P), 4)] for _, _, nk in UNITS]
GEND = [sum(len(g) for g in GROUPS[:i + 1]) for i in range(NU)]
NG = GEND[-1]
BOFF = [sum(u[2] for u in UNITS[:i]) for i in range(NU)]
NBIAS = sum(u[2] for u in UNITS)
HALVES = (64, 32, 16, 8, 4, 2)
NL = 5


def cols(j):
    return slice(j * JW, (j + 1) * JW)


class Signal:

    every = []

    def __init__(self, ctx, nc, name, per=1):
        self.sem, self.per = ctx.enter_context(nc.semaphore(name)), per
        Signal.every.append(self)

    def at(self, n, k=None):
        return (n + 3) * self.per if k is None else (n + 2) * self.per + k


class Chain:

    def __init__(self, eng, sem, base=0):
        self.eng, self.sem, self.base, self.n = eng, sem, base, 0

    def __call__(self, ins):
        self.n += 1
        ins.then_inc(self.sem, 1)
        self.eng.wait_ge(self.sem, self.base + self.n)


HOLD = []


def hold(eng):
    eng.sem_inc(HOLD[0], 1)


def in_pairs(eng, lo, hi, body):
    pairs = (hi - lo) // 2
    if pairs:
        hold(eng)
        with eng.Fori(0, pairs) as it:
            for s in range(2):
                body(2 * it + (lo + s), s, it + lo // 2)
    if (hi - lo) % 2:
        body(hi - 1, (hi - 1) % 2, (hi - 1) // 2)
    hold(eng)


def build(nc, io):
    ctx = ExitStack()
    Signal.every = []
    with ctx:
        made = []

        def sb(c, name, shape):
            made.append(name)
            again = made.count(name) - 1
            return c.enter_context(nc.sbuf_tensor(name + str(again) * bool(again), shape, F32))

        def sem(name):
            return ctx.enter_context(nc.semaphore(name))

        def sig(name, per=1):
            return Signal(ctx, nc, name, per)

        ident = sb(ctx, "ident", [P, P])
        ones = sb(ctx, "ones", [P, P])
        swapA = sb(ctx, "swapA", [P, P])
        swapB = sb(ctx, "swapB", [P, P])
        lmask = sb(ctx, "lmask", [P, NL, 32])
        bmask = sb(ctx, "bmask", [P, 4, 32])
        epst = sb(ctx, "epst", [P, 1])
        fgain = sb(ctx, "fgain", [P, KD])
        clow = sb(ctx, "clow", [D, L, HC])
        lower = sb(ctx, "lower", [D, L, HC])
        lbf = sb(ctx, "lbf", [D, L, HC])
        omlb = sb(ctx, "omlb", [D, L, HC])
        par = sb(ctx, "par", [P, PCOLS])
        neglam = sb(ctx, "neglam", [P, 1])
        xT = sb(ctx, "xT", [P, KD, T])
        PS = ctx.enter_context(nc.psum_tensor("PS", [P, 8, 512], F32))
        projT, projN = io["projT"], io["projN"]

        s_const, s_x = sem("s_const"), sem("s_x")
        HOLD[:] = [sem("waits_passed")]
        s_chain_setup, s_lowexp = sem("s_chain_setup"), sem("s_lowexp")
        s_par, s_lam, s_lamexp, s_chain_lam = sem("s_par"), sem("s_lam"), sem("s_lamexp"), sem("s_chain_lam")

        norm_sq, norm_used, norm_sum = sig("norm_sq", 8), sig("norm_used", 8), sig("norm_sum", 3)
        norm_root, norm_inv, norm_step = sig("norm_root"), sig("norm_inv"), sem("norm_step")
        pw_in = [sig("pw_in0", 16 * 10), sig("pw_in1", 16 * 9)]
        pt_mm, pt_ev = sig("pt_mm", 3), sig("pt_ev", 3)
        pt_swap, pt_sin, pt_cos, pt_sum = sig("pt_swap", 3), sig("pt_sin", 3), sig("pt_cos"), sig("pt_sum")
        pt_out = [sig("pt_out0", 16), sig("pt_out1", 16)]
        rope_in = sem("rope_in")
        pn_in = [sig("pn_in0", 16), sig("pn_in1", 16)]
        pn_mm, pn_ev = sig("pn_mm", 9), sig("pn_ev", 9)
        pn_out = [sig("pn_out0", 32), sig("pn_out1", 32)]
        ix_in, ix_dots, ix_relu, ix_acc = sem("ix_in"), sig("ix_dots", 28), sig("ix_relu", 28), sig("ix_acc", 28)
        ix_step, ix_pick = sem("ix_step"), sem("ix_pick")
        att = {}
        for g, maps in (("a", 2), ("b", 1)):
            att[g] = dict(
                inn=[sig(f"{g}_in0", 16 * 7), sig(f"{g}_in1", 16 * 7)], scores=sig(f"{g}_scores", NU * maps),
                negmax=sig(f"{g}_negmax", NU * maps), exp=sig(f"{g}_exp", NU * maps),
                comb=sig(f"{g}_comb", NU), tr=sig(f"{g}_tr", NG), ptc=sig(f"{g}_ptc", NG),
                pv=sig(f"{g}_pv", NU), tail=sig(f"{g}_tail"), step=sem(f"{g}_step"))
        c_in = [sig("c_in0", 16 * 5), sig("c_in1", 16 * 5)]
        c_gate, c_inv, c_q, c_x, c_ln = sig("c_gate", 2), sig("c_inv"), sig("c_q"), sig("c_x"), sig("c_ln")
        c_d, c_e, c_qm, c_km, c_last = sig("c_d", 10), sig("c_e", 10), sig("c_qm", 8), sig("c_km", 8), sig("c_last")
        c_att, c_attd, c_attc = sig("c_att", NU), sig("c_attd", NU), sig("c_attc", NU)
        c_o, c_su, c_s, c_tail = sig("c_o", NU), sig("c_su", NU), sig("c_s", NU), sig("c_tail")
        c_out = [sig("c_out0", 16), sig("c_out1", 16)]
        c_abs, c_dstep = sem("c_abs"), sem("c_dstep")
        mg_in, mg_sq, mg_ss, mg_root, mg_silu = sem("mg_in"), sem("mg_sq"), sem("mg_ss"), sem("mg_root"), sem("mg_silu")
        mg_step, mg_cat, mg_tr, mg_ev = sem("mg_step"), sem("mg_cat"), sig("mg_tr", 18), sig("mg_ev", 18)
        sig_add = {}
        for g in ("wo", "wd"):
            sig_add[g] = dict(inn=[sig(f"{g}_in0", 16), sig(f"{g}_in1", 16)], mm=sig(f"{g}_mm", 3), add=sig(f"{g}_add", 3))
        up_in = [sig("up_in0", 16), sig("up_in1", 16)]
        up_a, up_g, up_ev, up_conv = sig("up_a", 3), sig("up_g", 3), sig("up_ev", 3), sig("up_conv")
        up_silu, up_mul, up_step, up_zero = sig("up_silu"), sig("up_mul", 3), sem("up_step"), sem("up_zero")
        up_tail = sem("up_tail")
        s_y, s_yout = sem("s_y"), sem("s_yout")

        with nc.Block() as block:
            consts = [(ident, "ident"), (ones, "ones"), (swapA, "swapA"), (swapB, "swapB"), (lmask, "lmask"),
                      (bmask, "bmask"), (fgain, "fgain"), (clow, "clow")]

            @block.sync
            def _(sp):
                for t, name in consts:
                    sp.dma_start(t[:], io[name]).then_inc(s_const, 16)
                for k in range(KD):
                    sp.dma_start(xT[:, k, :], io["xT"][k * P:(k + 1) * P, :]).then_inc(s_x, 16)
                sp.wait_ge(s_const, 16 * len(consts))
                sp.wait_ge(s_x, 16 * KD)

            @block.gpsimd
            def _(pool):
                for s in Signal.every:
                    pool.sem_inc(s.sem, 2 * s.per)

            @block.scalar
            def _(act):
                act.wait_ge(s_chain_setup, 3)
                nc.scalar.activation(lower[:], lower[:], ACT.Exp).then_inc(s_lowexp, 1)

            @block.vector
            def _(dve):
                step = Chain(dve, s_chain_setup)
                step(nc.vector.memset(epst[:], EPS))
                dve.wait_ge(s_const, 16 * len(consts))
                mx, sm = omlb[:, 0, :], omlb[:, 1, :]
                step(nc.vector.tensor_tensor(mx, clow[:, 0, :], clow[:, 1, :], ALU.max))
                step(nc.vector.tensor_tensor(lower[:], clow[:], mx.unsqueeze(1).to_broadcast([D, L, HC]), ALU.subtract))
                dve.wait_ge(s_lowexp, 1)
                step(nc.vector.tensor_tensor(sm, lower[:, 0, :], lower[:, 1, :], ALU.add))
                step(nc.vector.reciprocal(mx, sm))
                step(nc.vector.tensor_tensor(lbf[:], lower[:], mx.unsqueeze(1).to_broadcast([D, L, HC]), ALU.mult))
                step(nc.vector.tensor_tensor(lower[:, 0, :], lbf[:, 0, :], lbf[:, 0, :], ALU.subtract))
                step(nc.vector.tensor_tensor(sm, lbf[:, 0, :], lbf[:, 1, :], ALU.add))
                step(nc.vector.tensor_tensor(lower[:, 1, :], sm, lbf[:, 0, :], ALU.subtract))
                step(nc.vector.tensor_scalar(omlb[:], lower[:], -1.0, 1.0, ALU.mult, ALU.add))
                step(nc.vector.tensor_scalar(lbf[:], lower[:], 1e-20, None, ALU.max))

        def rms_norm(n, gain, dst, extra=None):
            with ExitStack() as c:
                sq = sb(c, "sq", [P, 2, T])
                inv = sb(c, "inv", [P, T])
                with nc.Block() as block:
                    @block.scalar
                    def _(act):
                        for k in range(KD):
                            act.wait_ge(norm_used.sem, norm_used.at(n, k - 1))
                            nc.scalar.activation(sq[:, k % 2, :], xT[:, k, :], ACT.Square).then_inc(norm_sq.sem, 1)
                        act.wait_ge(norm_sum.sem, norm_sum.at(n))
                        nc.scalar.activation(inv[:].rearrange("p (j w) -> p j w", j=NJ), PS[:, 0:NJ, 0:JW], ACT.Sqrt,
                                             bias=epst[:], scale=1.0 / DM).then_inc(norm_root.sem, 1)

                    @block.tensor
                    def _(pe):
                        for k in range(KD):
                            pe.wait_ge(norm_sq.sem, norm_sq.at(n, k + 1))
                            for j in range(NJ):
                                mm = nc.tensor.matmul(PS[:, j, 0:JW], ones[:], sq[:, k % 2, cols(j)],
                                                      start=(k == 0), stop=(k == KD - 1))
                                if k == KD - 1:
                                    mm.then_inc(norm_sum.sem, 1)
                            if k < KD - 1:
                                mm.then_inc(norm_used.sem, 1)
                        pe.sem_inc(norm_used.sem, 1)

                    @block.vector
                    def _(dve):
                        dve.wait_ge(norm_root.sem, norm_root.at(n))
                        nc.vector.reciprocal(inv[:], inv[:]).then_inc(norm_inv.sem, 1)
                        dve.wait_ge(norm_inv.sem, norm_inv.at(n))
                        for k in range(KD):
                            nc.vector.scalar_tensor_tensor(dst[:, k, :], xT[:, k, :], gain[:, k:k + 1], inv[:],
                                                           ALU.mult, ALU.mult).then_inc(norm_step, 1)
                    if extra:
                        extra(block)

        def load_params(l):
            with nc.Block() as block:
                @block.sync
                def _(sp):
                    sp.dma_start(par[:], io["params"][bass.ds(l, 1)].rearrange("o p c -> p (o c)")).then_inc(s_par, 16)
                    sp.wait_ge(s_par, l * 16 + 16)
                    hold(sp)

                @block.scalar
                def _(act):
                    act.wait_ge(s_lam, l + 1)
                    nc.scalar.activation(par[:, P_LAM:P_LAM + 2], par[:, P_LAM:P_LAM + 2], ACT.Exp).then_inc(s_lamexp, 1)

                @block.vector
                def _(dve):
                    step = Chain(dve, s_chain_lam, l * 4)
                    dve.wait_ge(s_par, l * 16 + 16)
                    lam = par[:, P_LAM:P_LAM + 128].rearrange("p (m w d) -> p m w d", m=2, w=2)
                    prod = par[:, P_LAM + 64:P_LAM + 128].rearrange("p (m d) -> p m d", m=2)
                    step(nc.vector.tensor_tensor(par[:, P_LAM:P_LAM + 32], lam[:, 0, 0, :], lam[:, 0, 1, :], ALU.mult))
                    step(nc.vector.tensor_tensor(par[:, P_LAM + 32:P_LAM + 64], lam[:, 1, 0, :], lam[:, 1, 1, :], ALU.mult))
                    both = par[:, P_LAM:P_LAM + 64].rearrange("p (m d) -> p m d", m=2)
                    step(nc.vector.tensor_reduce(prod[:, 0, 0:2], both, AX, ALU.add))
                    nc.vector.tensor_copy(par[:, P_LAM:P_LAM + 2], prod[:, 0, 0:2]).then_inc(s_lam, 1)
                    dve.wait_ge(s_lamexp, l + 1)
                    step(nc.vector.tensor_tensor(neglam[:], par[:, P_LAM + 1:P_LAM + 2], par[:, P_LAM:P_LAM + 1], ALU.subtract))
                    nc.vector.tensor_tensor(neglam[:], neglam[:], par[:, P_LI:P_LI + 1], ALU.subtract)

        def project_features(l, xn):
            with ExitStack() as c:
                w = sb(c, "pw", [P, 2, KD, P])
                u = sb(c, "pu", [P, 2, T])
                tab = sb(c, "ptab", [P, 4, T])
                cosb = sb(c, "pcosb", [P, 2, T])
                out = sb(c, "pout", [P, 2, T])
                with nc.Block() as block:
                    def tiles(eng, rope, plain):
                        in_pairs(eng, 0, 6, lambda n, s, k: rope(n, s, k, 0, swapA, P))
                        in_pairs(eng, 6, 12, lambda n, s, k: rope(n, s, k, 2, swapB, P))
                        rope(12, 0, 6, 2, swapB, P)
                        rope(13, 1, 6, 2, swapB, 64)
                        in_pairs(eng, 14, NPT, lambda n, s, k: plain(n, s, k))

                    @block.sync
                    def _(sp):
                        for h in range(4):
                            sp.dma_start(tab[:, h, :], io["rope"][h]).then_inc(rope_in, 16)

                        def load(n, s, k):
                            N = l * NPT + n
                            sp.wait_ge(pt_mm.sem, pt_mm.at(N - 2))
                            sp.dma_start(w[:, s, :, :], io["wf"][bass.ds(l, 1), bass.ds(n, 1)]
                                         .rearrange("a b p (k c) -> p (a b k) c", c=P)).then_inc(pw_in[s].sem, 16)
                        in_pairs(sp, 0, NPT, load)

                    @block.tensor
                    def _(pe):
                        def main(n, s, k):
                            N = l * NPT + n
                            pe.wait_ge(pw_in[s].sem, pw_in[s].at(l, 16 * k + 16))
                            for j in range(NJ):
                                pe.wait_ge(pt_ev.sem, pt_ev.at(N - 2, j + 1))
                                for kk in range(KD):
                                    mm = nc.tensor.matmul(PS[:, 3 * s + j, 0:JW], w[:, s, kk, :], xn[:, kk, cols(j)],
                                                          start=(kk == 0), stop=(kk == KD - 1))
                                mm.then_inc(pt_mm.sem, 1)

                        def rope(n, s, k, t, swap, rows):
                            main(n, s, k)
                            R = l * 14 + n
                            for j in range(NJ):
                                b = 6 + j % 2
                                pe.wait_ge(pt_ev.sem, pt_ev.at(l * NPT + n, j + 1))
                                pe.wait_ge(pt_sin.sem, pt_sin.at(R, (0, -1, 1)[j]))
                                nc.tensor.matmul(PS[:, b, 0:JW], swap[:], u[:, s, cols(j)], start=True, stop=True)\
                                    .then_inc(pt_swap.sem, 1)
                        tiles(pe, rope, main)

                    @block.scalar
                    def _(act):
                        def evac(n, s, k):
                            N = l * NPT + n
                            for j in range(NJ):
                                act.wait_ge(pt_mm.sem, pt_mm.at(N, j + 1))
                                act.wait_ge(pt_sum.sem, pt_sum.at(N - 2))
                                nc.scalar.activation(u[:, s, cols(j)], PS[:, 3 * s + j, 0:JW], ACT.Copy)\
                                    .then_inc(pt_ev.sem, 1)
                            act.wait_ge(pt_sum.sem, pt_sum.at(N))
                            act.dma_start(projT[bass.ds(l, 1), bass.ds(n * P, P)].rearrange("a p t -> p (a t)"),
                                          out[:, s, :]).then_inc(pt_out[s].sem, 16)
                        tiles(act, lambda n, s, k, t, sw, r: evac(n, s, k), evac)
                        for s in range(2):
                            act.wait_ge(pt_out[s].sem, pt_out[s].at(l * (10 - s) + 9 - s))
                        hold(act)

                    @block.vector
                    def _(dve):
                        dve.wait_ge(rope_in, l * 64 + 64)
                        hold(dve)

                        def rope(n, s, k, t, swap, rows):
                            N, R = l * NPT + n, l * 14 + n
                            dve.wait_ge(pt_out[s].sem, pt_out[s].at(l * (10 - s) + k - 1))
                            for j in range(NJ):
                                dve.wait_ge(pt_swap.sem, pt_swap.at(R, j + 1))
                                nc.vector.tensor_tensor(out[:rows, s, cols(j)], PS[:rows, 6 + j % 2, 0:JW],
                                                        tab[:rows, t + 1, cols(j)], ALU.mult).then_inc(pt_sin.sem, 1)
                        tiles(dve, rope, lambda n, s, k: None)

                    @block.gpsimd
                    def _(pool):
                        pool.wait_ge(rope_in, l * 64 + 64)

                        def rope(n, s, k, t, swap, rows):
                            N, R = l * NPT + n, l * 14 + n
                            pool.wait_ge(pt_ev.sem, pt_ev.at(N))
                            nc.gpsimd.tensor_tensor(cosb[:rows, s, :], u[:rows, s, :], tab[:rows, t, :], ALU.mult)\
                                .then_inc(pt_cos.sem, 1)
                            pool.wait_ge(pt_cos.sem, pt_cos.at(R))
                            pool.wait_ge(pt_sin.sem, pt_sin.at(R))
                            if rows < P:
                                pool.wait_ge(pt_out[s].sem, pt_out[s].at(l * (10 - s) + k - 1))
                                hold(pool)
                                nc.gpsimd.tensor_copy(out[rows:, s, :], u[rows:, s, :])
                            nc.gpsimd.tensor_tensor(out[:rows, s, :], out[:rows, s, :], cosb[:rows, s, :], ALU.add)\
                                .then_inc(pt_sum.sem, 1)

                        def plain(n, s, k):
                            N = l * NPT + n
                            pool.wait_ge(pt_ev.sem, pt_ev.at(N))
                            pool.wait_ge(pt_out[s].sem, pt_out[s].at(l * (10 - s) + k - 1))
                            hold(pool)
                            nc.gpsimd.tensor_copy(out[:, s, :], u[:, s, :]).then_inc(pt_sum.sem, 1)
                        tiles(pool, rope, plain)

        def project_tokens(l, xn):
            with ExitStack() as c:
                w = sb(c, "nw", [P, 2, KD, CW])
                out = sb(c, "nout", [P, 2, NT + 1, CW])
                with nc.Block() as block:
                    @block.sync
                    def _(sp):
                        def load(n, s, k):
                            N = l * NC4 + n
                            sp.wait_ge(pn_mm.sem, pn_mm.at(N - 2))
                            sp.dma_start(w[:, s, :, :], io["wn"][bass.ds(l, 1), bass.ds(n, 1)]
                                         .rearrange("a b p (k c) -> p (a b k) c", c=CW)).then_inc(pn_in[s].sem, 16)
                        in_pairs(sp, 0, NC4, load)

                    @block.tensor
                    def _(pe):
                        def chunk(n, s, k):
                            N = l * NC4 + n
                            pe.wait_ge(pn_in[s].sem, pn_in[s].at(l * 2 + k))
                            for i in range(NU):
                                q0, nq, _ = UNITS[i]
                                pe.wait_ge(pn_ev.sem, pn_ev.at(N, i - 3) if i >= 4 else pn_ev.at(N - 2))
                                for kk in range(KD):
                                    mm = nc.tensor.matmul(PS[:nq, 4 * s + i % 4, 0:CW], xn[:, kk, q0:q0 + nq], w[:, s, kk, :],
                                                          start=(kk == 0), stop=(kk == KD - 1))
                                mm.then_inc(pn_mm.sem, 1)
                        in_pairs(pe, 0, NC4, chunk)

                    @block.scalar
                    def _(act):
                        def evac(n, s, k):
                            N = l * NC4 + n
                            act.wait_ge(pn_out[s].sem, pn_out[s].at(l * 2 + k - 1))
                            for i in range(NU):
                                nq = UNITS[i][1]
                                act.wait_ge(pn_mm.sem, pn_mm.at(N, i + 1))
                                nc.scalar.activation(out[:nq, s, i, :], PS[:nq, 4 * s + i % 4, 0:CW], ACT.Copy)\
                                    .then_inc(pn_ev.sem, 1)
                            act.wait_ge(pn_ev.sem, pn_ev.at(N))
                            rows = projN[bass.ds(l, 1), :, bass.ds(n * CW, CW)]
                            act.dma_start(rows[:, 0:TP, :].rearrange("a (i p) c -> p (a i) c", p=P),
                                           out[:, s, 0:NT, :]).then_inc(pn_out[s].sem, 16)
                            act.dma_start(rows[:, TP:T, :].rearrange("a p c -> p (a c)"),
                                           out[:TS, s, NT, :]).then_inc(pn_out[s].sem, 16)
                        in_pairs(act, 0, NC4, evac)
                        for s in range(2):
                            act.wait_ge(pn_out[s].sem, pn_out[s].at(l * 2 + 1))
                        hold(act)

        def index_scores(l, bias):
            units = list(range(2, NU))
            rounds = [TOP_P // 8] * (len(units) - 1) + [TOP_S // 8]
            total = 2 * sum(rounds)
            with ExitStack() as c:
                iq = sb(c, "iq", [D, HI, T])
                ik = sb(c, "ik", [D, T + PAST])
                iw = sb(c, "iw", [P, NU, HI])
                rl = sb(c, "rl", [P, 2, TP])
                work = sb(c, "work", [P, TP])
                top = sb(c, "top", [P, 8])
                nload = 6
                with nc.Block() as block:
                    @block.sync
                    def _(sp):
                        pt = projT[bass.ds(l, 1)]
                        pn = projN[bass.ds(l, 1), :, C_IW:C_IW + HI]
                        for dst, src in (
                                (iq[:], pt[:, R_IQ:R_IQ + HI * D, :].rearrange("a (h p) t -> p (a h) t", p=D)),
                                (ik[:, 0:TP], pt[:, R_IK:R_IK + D, 0:TP].rearrange("a p t -> p (a t)")),
                                (ik[:, TP + PAST:], pt[:, R_IK:R_IK + D, TP:T].rearrange("a p t -> p (a t)")),
                                (ik[:, TP:TP + PAST], io["kidx"][bass.ds(l, 1)].rearrange("a p t -> p (a t)")),
                                (iw[:, 0:NT, :], pn[:, 0:TP, :].rearrange("a (i p) c -> p (a i) c", p=P)),
                                (iw[:TS, NT, :], pn[:, TP:T, :].rearrange("a p c -> p (a c)"))):
                            sp.dma_start(dst, src).then_inc(ix_in, 16)
                        sp.wait_ge(ix_in, (l + 1) * 16 * nload)
                        hold(sp)

                    @block.tensor
                    def _(pe):
                        pe.wait_ge(ix_in, (l + 1) * 16 * nload)
                        for y, i in enumerate(units):
                            q0, nq, nk = UNITS[i]
                            for h in range(HI):
                                pe.wait_ge(ix_relu.sem, ix_relu.at(l, 4 * y + h - 1))
                                hold(pe)
                                for a in range(0, nk, 512):
                                    b = min(nk, a + 512)
                                    mm = nc.tensor.matmul(PS[:nq, 2 * (h % 2) + a // 512, 0:b - a], iq[:, h, q0:q0 + nq],
                                                          ik[:, KEY0[i] + a:KEY0[i] + b], start=True, stop=True)
                                mm.then_inc(ix_dots.sem, 1)

                    @block.scalar
                    def _(act):
                        for y, i in enumerate(units):
                            q0, nq, nk = UNITS[i]
                            for h in range(HI):
                                act.wait_ge(ix_dots.sem, ix_dots.at(l, 4 * y + h + 1))
                                act.wait_ge(ix_acc.sem, ix_acc.at(l, 4 * y + h - 1))
                                src = PS[:nq, 2 * (h % 2):2 * (h % 2) + 2, :].rearrange("p b w -> p (b w)")[:, 0:nk]
                                nc.scalar.activation(rl[:nq, h % 2, 0:nk], src, ACT.Relu, scale=D ** -0.5)\
                                    .then_inc(ix_relu.sem, 1)

                    @block.vector
                    def _(dve):
                        isteps = 3 + 2 * len(units) - 1
                        step = Chain(dve, ix_step, l * isteps)
                        dve.wait_ge(ix_in, (l + 1) * 16 * nload)
                        nc.vector.tensor_scalar(iw[:, 0:NT, :], iw[:, 0:NT, :], HI ** -0.5, None, ALU.mult)
                        step(nc.vector.tensor_scalar(iw[:TS, NT, :], iw[:TS, NT, :], HI ** -0.5, None, ALU.mult))
                        for i in range(2):
                            step(nc.vector.memset(bias[:, BOFF[i]:BOFF[i + 1]], 0.0))
                            nc.vector.memset(bias[0:64, BOFF[i + 1] - 64:BOFF[i + 1]], 8 * NEG)
                        done = 0
                        for y, i in enumerate(units):
                            q0, nq, nk = UNITS[i]
                            wk = work[:nq, 0:nk]
                            for h in range(HI):
                                dve.wait_ge(ix_relu.sem, ix_relu.at(l, 4 * y + h + 1))
                                if h == 0:
                                    nc.vector.tensor_scalar(wk, rl[:nq, 0, 0:nk], iw[:nq, i, 0:1], None, ALU.mult)\
                                        .then_inc(ix_acc.sem, 1)
                                else:
                                    dve.wait_ge(ix_acc.sem, ix_acc.at(l, 4 * y + h))
                                    nc.vector.scalar_tensor_tensor(wk, rl[:nq, h % 2, 0:nk], iw[:nq, i, h:h + 1], wk,
                                                                   ALU.mult, ALU.add).then_inc(ix_acc.sem, 1)
                            dve.wait_ge(ix_acc.sem, ix_acc.at(l, 4 * y + 4))
                            if i < NT:
                                step(nc.vector.memset(work[0:64, nk - 64:nk], NEG))

                            def pick(base):
                                nc.vector.max(top[:nq, :], wk).then_inc(ix_pick, 1)
                                dve.wait_ge(ix_pick, base + 1)
                                hold(dve)
                                nc.vector.match_replace(wk, top[:nq, :], wk, SENTINEL).then_inc(ix_pick, 1)
                                dve.wait_ge(ix_pick, base + 2)
                                hold(dve)
                            r = rounds[y]
                            hold(dve)
                            with dve.Fori(0, r // 4) as it:
                                for z in range(4):
                                    pick(it * 8 + l * total + (done + 2 * z))
                            for z in range(r // 4 * 4, r):
                                pick(l * total + done + 2 * z)
                            done += 2 * r
                            step(nc.vector.tensor_scalar(bias[:nq, BOFF[i]:BOFF[i] + nk], wk, SENTINEL, 8 * NEG,
                                                         ALU.not_equal, ALU.mult))
                        assert step.n == isteps
                        hold(dve)

        def attention(l, g, heads, maps, cat, col0, bias=None):
            S = att[g]
            hw = D // maps
            scale = hw ** -0.5
            rq, rk, cv = (R_AQ, R_AK, C_AV) if g == "a" else (R_BQ, R_BK, C_BV)
            prev = {0: 0, 1: -1}
            done_before = [prev.get(i, i - 1) for i in range(NU)]
            gdone = [0, GEND[7] - NG] + [GEND[i - 2] for i in range(2, NU)]
            steps = 2 * NT + 2 * NU + 3 * NU if g == "a" else NU + 2
            with ExitStack() as c:
                q = sb(c, f"{g}q", [D, 2, T])
                kb = sb(c, f"{g}k", [D, 2, T + PAST])
                v = sb(c, f"{g}v", [P, 2, NT + 5, D])
                pm = sb(c, f"{g}p", [P, 2, maps, TP])
                cb = sb(c, f"{g}c", [P, 2, TP]) if g == "a" else pm[:, :, 0, :]
                pt = sb(c, f"{g}pt", [P, 2, NT, P])
                mx = sb(c, f"{g}mx", [P, NU, maps])
                ngm = sb(c, f"{g}ngm", [P, NU, maps])
                sums = sb(c, f"{g}sums", [P, NU, maps])
                rs = sb(c, f"{g}rs", [P, NU, maps])

                def bank(i, m):
                    return 2 * (m if maps == 2 else i % 2)

                def scores_of(i, m):
                    b = bank(i, m)
                    return PS[:UNITS[i][1], b:b + 2, :].rearrange("p b w -> p (b w)")[:, 0:UNITS[i][2]]

                with nc.Block() as block:
                    @block.sync
                    def _(sp):
                        def load(h, s, k):
                            n = l * heads + h
                            sp.wait_ge(S["pv"].sem, S["pv"].at(n - 2))
                            pt_ = projT[bass.ds(l, 1)]
                            pn = projN[bass.ds(l, 1), :, bass.ds(h * D + cv, D)]
                            rows = lambda r: pt_[:, bass.ds(h * D + r, D), :].rearrange("a p t -> p (a t)")
                            for dst, src in (
                                    (q[:, s, :], rows(rq)),
                                    (kb[:, s, 0:TP], rows(rk)[:, 0:TP]),
                                    (kb[:, s, TP + PAST:], rows(rk)[:, TP:T]),
                                    (kb[:, s, TP:TP + PAST], io[g + "k"][bass.ds(l, 1), bass.ds(h, 1)].rearrange("a b p t -> p (a b t)")),
                                    (v[:, s, 0:NT, :], pn[:, 0:TP, :].rearrange("a (i p) c -> p (a i) c", p=P)),
                                    (v[:, s, NT:NT + 4, :], io[g + "v"][bass.ds(l, 1), bass.ds(h, 1)].rearrange("a b p i c -> p (a b i) c")),
                                    (v[:TS, s, NT + 4, :], pn[:, TP:T, :].rearrange("a p c -> p (a c)"))):
                                sp.dma_start(dst, src).then_inc(S["inn"][s].sem, 16)
                        in_pairs(sp, 0, heads, load)

                    @block.tensor
                    def _(pe):
                        def head(h, s, k):
                            n = l * heads + h
                            pe.wait_ge(S["inn"][s].sem, S["inn"][s].at(l * ((heads + 1 - s) // 2) + k))

                            def score(i):
                                q0, nq, nk = UNITS[i]
                                for m in range(maps):
                                    if maps == 2:
                                        pe.wait_ge(S["exp"].sem, S["exp"].at(n, 2 * i + m - 1))
                                    else:
                                        pe.wait_ge(S["negmax"].sem, S["negmax"].at(n, done_before[i]))
                                    hold(pe)
                                    r = slice(hw * m, hw * (m + 1))
                                    for a in range(0, nk, 512):
                                        b = min(nk, a + 512)
                                        mm = nc.tensor.matmul(PS[:nq, bank(i, m) + a // 512, 0:b - a], q[r, s, q0:q0 + nq],
                                                              kb[r, s, KEY0[i] + a:KEY0[i] + b], start=True, stop=True)
                                    mm.then_inc(S["scores"].sem, 1)

                            def turn(i):
                                q0, nq, nk = UNITS[i]
                                pe.wait_ge(S["comb" if g == "a" else "exp"].sem, S["comb" if g == "a" else "exp"].at(n, i + 1))
                                g0 = GEND[i] - len(GROUPS[i])
                                for z, grp in enumerate(GROUPS[i]):
                                    pe.wait_ge(S["ptc"].sem, S["ptc"].at(n, g0 + z - 1))
                                    hold(pe)
                                    for kt in grp:
                                        kw = min(P, nk - kt * P)
                                        mm = nc.tensor.transpose(PS[:kw, 4 + (g0 + z) % 2, (kt % 4) * P:(kt % 4) * P + nq],
                                                                 cb[:nq, i % 2, kt * P:kt * P + kw], ident[:nq, :nq])
                                    mm.then_inc(S["tr"].sem, 1)
                                pe.wait_ge(S["ptc"].sem, S["ptc"].at(n, GEND[i]))
                                if i == 0:
                                    pe.wait_ge(S["tail"].sem, S["tail"].at(n - 1))
                                hold(pe)
                                last = -(-nk // P) - 1
                                dst = PS[:nq, 6, i * D:(i + 1) * D] if i < NT else PS[:nq, 7, 0:D]
                                for kt in range(last + 1):
                                    kw = min(P, nk - kt * P)
                                    mm = nc.tensor.matmul(dst, pt[:kw, i % 2, kt, 0:nq], v[:kw, s, VT0[i] + kt, :],
                                                          start=(kt == 0), stop=(kt == last))
                                mm.then_inc(S["pv"].sem, 1)
                            score(0)
                            for i in range(1, NU):
                                score(i)
                                turn(i - 1)
                            turn(NU - 1)
                        in_pairs(pe, 0, heads, head)

                    @block.scalar
                    def _(act):
                        def head(h, s, k):
                            n = l * heads + h

                            def expo(i):
                                q0, nq, nk = UNITS[i]
                                for m in range(maps):
                                    act.wait_ge(S["negmax"].sem, S["negmax"].at(n, maps * i + m + 1))
                                    if maps == 2:
                                        act.wait_ge(S["comb"].sem, S["comb"].at(n, done_before[i]))
                                    src = scores_of(i, m) if maps == 2 else pm[:nq, i % 2, 0, 0:nk]
                                    nc.scalar.activation(pm[:nq, i % 2, m, 0:nk], src, ACT.Exp, bias=ngm[:nq, i, m:m + 1],
                                                         scale=scale if maps == 2 else 1.0,
                                                         accum_out=sums[:nq, i, m:m + 1]).then_inc(S["exp"].sem, 1)

                            def copies(i):
                                q0, nq, nk = UNITS[i]
                                g0 = GEND[i] - len(GROUPS[i])
                                act.wait_ge(S["pv"].sem, S["pv"].at(n, done_before[i]))
                                for z, grp in enumerate(GROUPS[i]):
                                    act.wait_ge(S["tr"].sem, S["tr"].at(n, g0 + z + 1))
                                    kw = min(P, nk - grp[0] * P)
                                    src = PS[:kw, 4 + (g0 + z) % 2, 0:len(grp) * P].rearrange("p (t w) -> p t w", w=P)
                                    nc.scalar.activation(pt[:kw, i % 2, grp[0]:grp[-1] + 1, 0:nq], src[:, :, 0:nq], ACT.Copy)\
                                        .then_inc(S["ptc"].sem, 1)
                            expo(0)
                            for i in range(1, NU):
                                expo(i)
                                copies(i - 1)
                            copies(NU - 1)
                        in_pairs(act, 0, heads, head)

                    @block.vector
                    def _(dve):
                        def head(h, s, k):
                            n = l * heads + h
                            step = Chain(dve, S["step"], n * steps)

                            def maxima(i):
                                q0, nq, nk = UNITS[i]
                                for m in range(maps):
                                    dve.wait_ge(S["scores"].sem, S["scores"].at(n, maps * i + m + 1))
                                    if g == "a":
                                        sc = scores_of(i, m)
                                        if i < NT:
                                            b = bank(i, m) * 512 + nk - 64
                                            step(nc.vector.memset(PS[0:64, b // 512, b % 512:b % 512 + 64], NEG))
                                        step(nc.vector.tensor_reduce(mx[:nq, i, m:m + 1], sc, AX, ALU.max))
                                        nc.vector.tensor_scalar(ngm[:nq, i, m:m + 1], mx[:nq, i, m:m + 1], -scale, None, ALU.mult)\
                                            .then_inc(S["negmax"].sem, 1)
                                    else:
                                        dve.wait_ge(S["tr"].sem, S["tr"].at(n, gdone[i]))
                                        hold(dve)
                                        step(nc.vector.tensor_tensor_reduce(
                                            out=pm[:nq, i % 2, 0, 0:nk], in0=scores_of(i, 0), in1=bias[:nq, BOFF[i]:BOFF[i] + nk],
                                            scale=scale, scalar=-3.4e38, op0=ALU.add, op1=ALU.max, accum_out=mx[:nq, i, 0:1]))
                                        nc.vector.tensor_scalar(ngm[:nq, i, 0:1], mx[:nq, i, 0:1], -1.0, None, ALU.mult)\
                                            .then_inc(S["negmax"].sem, 1)

                            def combine(i):
                                q0, nq, nk = UNITS[i]
                                dve.wait_ge(S["exp"].sem, S["exp"].at(n, 2 * i + 2))
                                step(nc.vector.reciprocal(rs[:nq, i, :], sums[:nq, i, :]))
                                step(nc.vector.tensor_tensor(rs[:nq, i, 1:2], rs[:nq, i, 1:2], neglam[:nq, :], ALU.mult))
                                step(nc.vector.tensor_scalar(pm[:nq, i % 2, 1, 0:nk], pm[:nq, i % 2, 1, 0:nk], rs[:nq, i, 1:2],
                                                             None, ALU.mult))
                                dve.wait_ge(S["tr"].sem, S["tr"].at(n, gdone[i]))
                                nc.vector.scalar_tensor_tensor(cb[:nq, i % 2, 0:nk], pm[:nq, i % 2, 0, 0:nk], rs[:nq, i, 0:1],
                                                               pm[:nq, i % 2, 1, 0:nk], ALU.mult, ALU.add)\
                                    .then_inc(S["comb"].sem, 1)
                            maxima(0)
                            for i in range(1, NU):
                                maxima(i)
                                if g == "a":
                                    combine(i - 1)
                            if g == "a":
                                combine(NU - 1)
                            dve.wait_ge(S["pv"].sem, S["pv"].at(n))
                            o = PS[:, 6, :].rearrange("p (i d) -> p i d", d=D)
                            oc = cat[:, :, bass.ds(h * D + col0, D)]
                            if g == "a":
                                nc.vector.tensor_copy(oc[:, 0:NT, :], o)
                                nc.vector.tensor_copy(oc[:TS, NT, :], PS[:TS, 7, 0:D]).then_inc(S["tail"].sem, 1)
                            else:
                                dve.wait_ge(S["exp"].sem, S["exp"].at(n))
                                step(nc.vector.reciprocal(rs[:, 0:NT, 0], sums[:, 0:NT, 0]))
                                step(nc.vector.reciprocal(rs[:TS, NT, :], sums[:TS, NT, :]))
                                nc.vector.tensor_tensor(oc[:, 0:NT, :], o, rs[:, 0:NT, :].to_broadcast([P, NT, D]), ALU.mult)
                                nc.vector.tensor_scalar(oc[:TS, NT, :], PS[:TS, 7, 0:D], rs[:TS, NT, :], None, ALU.mult)\
                                    .then_inc(S["tail"].sem, 1)
                            assert step.n == steps
                        in_pairs(dve, 0, heads, head)

        def hgrn(l, cat, col0):
            with ExitStack() as c:
                zq = sb(c, "zq", [D, 2, T])
                zf = sb(c, "zf", [D, 2, T])
                v = sb(c, "cv", [P, 2, NU, D])
                s0 = sb(c, "s0", [D, 2, D])
                sout = sb(c, "sout", [D, 2, 2, D])
                eq = sb(c, "eq", [D, T])
                ef = sb(c, "ef", [D, T])
                sg = sb(c, "sg", [D, T])
                x2 = sb(c, "x2", [D, T])
                kk_ = sb(c, "ck", [D, T])
                b = sb(c, "cb", [D, T])
                e = sb(c, "ce", [D, 2, T])
                qL = sb(c, "qL", [D, 7, T])
                kL = sb(c, "kL", [D, 7, T])
                qe = sb(c, "qe", [D, T])
                kd = sb(c, "kd", [D, T])
                ebl = sb(c, "ebl", [D, NU])
                lc = sb(c, "lc", [D, 2, HC])
                lh = sb(c, "lh", [D, 2])
                st = sb(c, "st", [D, 2, D])
                kdT = sb(c, "kdT", [P, 2, D])
                md = sb(c, "md", [P, NL, 32])
                ad = sb(c, "ad", [P, 32])
                at_ = sb(c, "at", [P, 2, P])
                DSTEPS = 9 + NU + NT
                qi = {0: 1, 2: 2, 3: 3, 4: 4, 5: 5, 6: 6, 7: 7, 8: 8}
                ki = {1: 1, 2: 2, 3: 3, 4: 4, 5: 5, 6: 6, 7: 7, 9: 8}

                def span(item):
                    return TP if item in (2, 3) else T

                with nc.Block() as block:
                    @block.sync
                    def _(sp):
                        def load(h, s, k):
                            n = l * HC + h
                            sp.wait_ge(c_o.sem, c_o.at(n - 2))
                            sp.wait_ge(c_s.sem, c_s.at(n - 2))
                            pt_ = projT[bass.ds(l, 1)]
                            pn = projN[bass.ds(l, 1), :, bass.ds(h * D + C_CI, D)]
                            rows = lambda r: pt_[:, bass.ds(h * D + r, D), :].rearrange("a p t -> p (a t)")
                            for dst, src in (
                                    (zq[:, s, :], rows(R_CQ)), (zf[:, s, :], rows(R_CF)),
                                    (v[:, s, 0:NT, :], pn[:, 0:TP, :].rearrange("a (i p) c -> p (a i) c", p=P)),
                                    (v[:TS, s, NT, :], pn[:, TP:T, :].rearrange("a p c -> p (a c)")),
                                    (s0[:, s, :], io["s0"][bass.ds(l, 1), bass.ds(h, 1)].rearrange("a b p c -> p (a b c)"))):
                                sp.dma_start(dst, src).then_inc(c_in[s].sem, 16)
                        in_pairs(sp, 0, HC, load)

                    @block.scalar
                    def _(act):
                        def head(h, s, k):
                            n = l * HC + h
                            act.wait_ge(c_in[s].sem, c_in[s].at(l * ((HC + 1 - s) // 2) + k))
                            act.wait_ge(c_q.sem, c_q.at(n - 1))
                            nc.scalar.activation(eq[:], zq[:, s, :], ACT.Exp, scale=-1.0).then_inc(c_gate.sem, 1)
                            act.wait_ge(c_km.sem, c_km.at(n - 1))
                            nc.scalar.activation(ef[:], zf[:, s, :], ACT.Exp, scale=-1.0).then_inc(c_gate.sem, 1)
                            act.wait_ge(c_x.sem, c_x.at(n))
                            nc.scalar.activation(sg[:], sg[:], ACT.Ln)
                            nc.scalar.activation(x2[:], x2[:], ACT.Ln).then_inc(c_ln.sem, 1)
                            act.wait_ge(c_d.sem, c_d.at(n, 1))
                            act.wait_ge(c_s.sem, c_s.at(n - 1))
                            nc.scalar.activation(ebl[:, 0:NT], b[:, 0:TP].rearrange("p (i w) -> p i w", w=P)[:, :, P - 1], ACT.Exp)
                            nc.scalar.activation(ebl[:, NT:NU], b[:, T - 1:T], ACT.Exp).then_inc(c_last.sem, 1)
                            for item in range(10):
                                w = span(item)
                                act.wait_ge(c_d.sem, c_d.at(n, item + 1))
                                buf = e[:, item % 2, 0:w]
                                if item == 0:
                                    act.wait_ge(c_km.sem, c_km.at(n - 1))
                                    nc.scalar.activation(buf, b[:], ACT.Exp).then_inc(c_e.sem, 1)
                                elif item in (1, 8, 9):
                                    nc.scalar.activation(buf, buf, ACT.Exp).then_inc(c_e.sem, 1)
                                else:
                                    nc.scalar.activation(buf, buf, ACT.Abs).then_inc(c_abs, 1)
                                    act.wait_ge(c_abs, n * 6 + (item - 1))
                                    nc.scalar.activation(buf, buf, ACT.Exp, scale=-1.0).then_inc(c_e.sem, 1)
                            for t in range(NU):
                                act.wait_ge(c_att.sem, c_att.at(n, t + 1))
                                act.wait_ge(c_su.sem, c_su.at(n, {0: 0, 1: -1}.get(t, t - 1)))
                                act.wait_ge(c_attd.sem, c_attd.at(n, t + 1))
                                w = UNITS[t][1]
                                src = PS[:, t % 2, :]
                                if t < NT:
                                    nc.scalar.activation(at_[0:64, t % 2, 64:128], src[0:64, 0:64], ACT.Copy)
                                    nc.scalar.activation(at_[0:32, t % 2, 32:64], src[0:32, 64:96], ACT.Copy)
                                    nc.scalar.activation(at_[64:96, t % 2, 96:128], src[64:96, 64:96], ACT.Copy)
                                nc.scalar.activation(kdT[:w, t % 2, :], PS[:w, 2 + t % 2, 0:D], ACT.Copy).then_inc(c_attc.sem, 1)
                            act.wait_ge(c_s.sem, c_s.at(n))
                            act.dma_start(io["stateC"][bass.ds(l, 1), bass.ds(h, 1)].rearrange("a b p m c -> p (a b m) c"),
                                          sout[:, s, :, :]).then_inc(c_out[s].sem, 16)
                        in_pairs(act, 0, HC, head)
                        for s in range(2):
                            act.wait_ge(c_out[s].sem, c_out[s].at(l * ((HC + 1 - s) // 2) + (HC + 1 - s) // 2 - 1))
                        hold(act)

                    @block.gpsimd
                    def _(pool):
                        def head(h, s, k):
                            n = l * HC + h
                            pool.wait_ge(c_inv.sem, c_inv.at(n))
                            nc.gpsimd.tensor_tensor(eq[:], zq[:, s, :], eq[:], ALU.mult).then_inc(c_q.sem, 1)
                            pool.wait_ge(c_q.sem, c_q.at(n))
                            pool.wait_ge(c_att.sem, c_att.at(n - 1))
                            pool.wait_ge(c_o.sem, c_o.at(n - 1))
                            for item in range(10):
                                if item not in qi:
                                    continue
                                w = span(item)
                                pool.wait_ge(c_e.sem, c_e.at(n, item + 1))
                                dst = qe[:] if item == 0 else qL[:, item - 2, 0:w]
                                nc.gpsimd.tensor_tensor(dst, eq[:, 0:w], e[:, item % 2, 0:w], ALU.mult).then_inc(c_qm.sem, 1)
                        in_pairs(pool, 0, HC, head)

                    @block.vector
                    def _(dve):
                        step = Chain(dve, c_dstep, l * (1 + HC * DSTEPS))
                        nc.vector.tensor_copy(lc[:, 0, :], lbf[:, bass.ds(l, 1), :].rearrange("p a h -> p (a h)"))
                        step(nc.vector.tensor_copy(lc[:, 1, :], omlb[:, bass.ds(l, 1), :].rearrange("p a h -> p (a h)")))

                        def head(h, s, k):
                            n = l * HC + h
                            step = Chain(dve, c_dstep, l * (1 + HC * DSTEPS) + (h * DSTEPS + 1))
                            step(nc.vector.tensor_copy(lh[:], lc[:, :, bass.ds(h, 1)].rearrange("p a h -> p (a h)")))
                            dve.wait_ge(c_gate.sem, c_gate.at(n, 1))
                            step(nc.vector.tensor_scalar(eq[:], eq[:], 3e38, 1.0, ALU.min, ALU.add))
                            nc.vector.reciprocal(eq[:], eq[:]).then_inc(c_inv.sem, 1)
                            dve.wait_ge(c_gate.sem, c_gate.at(n, 2))
                            step(nc.vector.tensor_scalar(ef[:], ef[:], 1e30, None, ALU.min))
                            step(nc.vector.tensor_scalar(sg[:], ef[:], 1.0, None, ALU.add))
                            step(nc.vector.reciprocal(sg[:], sg[:]))
                            step(nc.vector.scalar_tensor_tensor(kk_[:], ef[:], lh[:, 1:2], sg[:], ALU.mult, ALU.mult))
                            step(nc.vector.tensor_scalar(sg[:], sg[:], lh[:, 1:2], lh[:, 0:1], ALU.mult, ALU.add))
                            step(nc.vector.tensor_scalar(x2[:], sg[:], 2.0 ** 60, 1.0, ALU.mult, ALU.min))
                            nc.vector.tensor_scalar(sg[:], sg[:], 2.0 ** -60, None, ALU.max).then_inc(c_x.sem, 1)
                            dve.wait_ge(c_ln.sem, c_ln.at(n))
                            for t in range(NU):
                                q0, w, _ = UNITS[t]
                                r = slice(q0, q0 + w)
                                ins = nc.vector.tensor_tensor_scan(b[:, r], sg[:, r], x2[:, r], 0.0, ALU.add, ALU.add)
                            ins.then_inc(c_d.sem, 1)
                            dve.wait_ge(c_d.sem, c_d.at(n, 1))
                            dve.wait_ge(c_attc.sem, c_attc.at(n - 1))

                            def diff(item):
                                if item >= 2:
                                    dve.wait_ge(c_qm.sem, c_qm.at(n, qi.get(item - 2, 1 if item == 3 else 8)))
                                    if item - 2 in ki:
                                        dve.wait_ge(c_km.sem, c_km.at(n, ki[item - 2]))
                                w = span(item)
                                if item == 1:
                                    bt = b[:, 0:TP].rearrange("p (i w) -> p i w", w=P)
                                    nc.vector.tensor_tensor(e[:, 1, 0:TP].rearrange("p (i w) -> p i w", w=P),
                                                            bt[:, :, P - 1:P].to_broadcast([D, NT, P]), bt, ALU.subtract)
                                    nc.vector.tensor_tensor(e[:, 1, TP:T], b[:, T - 1:T].to_broadcast([D, TS]), b[:, TP:T],
                                                            ALU.subtract).then_inc(c_d.sem, 1)
                                    return
                                hw, r = (HALVES[item - 2], HALVES[item - 2] - 1) if item < 8 else (1, 0)
                                bt = b[:, 0:w].rearrange("p (i w) -> p i w", w=2 * hw)
                                ref = bt[:, :, r:r + 1].to_broadcast([D, w // (2 * hw), 2 * hw])
                                ins = (ref, bt) if item == 9 else (bt, ref)
                                nc.vector.tensor_tensor(e[:, item % 2, 0:w].rearrange("p (i w) -> p i w", w=2 * hw),
                                                        ins[0], ins[1], ALU.subtract).then_inc(c_d.sem, 1)

                            def kmul(item):
                                if item not in ki:
                                    return
                                w = span(item)
                                dve.wait_ge(c_e.sem, c_e.at(n, item + 1))
                                dst = kd[:] if item == 1 else kL[:, min(item, 8) - 2, 0:w]
                                nc.vector.tensor_tensor(dst, kk_[:, 0:w], e[:, item % 2, 0:w], ALU.mult).then_inc(c_km.sem, 1)
                            diff(1)
                            for item in range(2, 10):
                                diff(item)
                                kmul(item - 1)
                            kmul(9)
                            step(nc.vector.memset(st[:, 0, :], 0.0))
                            dve.wait_ge(c_last.sem, c_last.at(n))
                            dve.wait_ge(c_out[s].sem, c_out[s].at(l * ((HC + 1 - s) // 2) + k - 1))
                            for t in range(NU):
                                w = UNITS[t][1]
                                dve.wait_ge(c_att.sem, c_att.at(n, t + 1))
                                dve.wait_ge(c_o.sem, c_o.at(n, {0: 0, 1: -1}.get(t, t - 1)))
                                pd = PS[:w, t % 2, 96:96 + NL * 32].rearrange("p (l w) -> p l w", w=32)
                                step(nc.vector.tensor_tensor(md[:w], pd, lmask[:w], ALU.mult))
                                red = at_[:w, t % 2, 0:32] if t == NT else ad[:]
                                ins = nc.vector.tensor_reduce(red, md[:w].rearrange("p l w -> p w l"), AX, ALU.add)
                                if t < NT:
                                    step(ins)
                                    ins = nc.vector.tensor_tensor(at_[:, t % 2, :].rearrange("p (j w) -> p j w", w=32),
                                                                  ad[:].unsqueeze(1).to_broadcast([P, 4, 32]), bmask[:], ALU.mult)
                                ins.then_inc(c_attd.sem, 1)
                                dve.wait_ge(c_su.sem, c_su.at(n, t + 1))
                                if t > 0:
                                    dve.wait_ge(c_s.sem, c_s.at(n, t))
                                src = st[:, t % 2, :] if t < NT else s0[:, s, :]
                                dst = st[:, (t + 1) % 2, :] if t < NT - 1 else sout[:, s, t - NT + 1, :]
                                nc.vector.scalar_tensor_tensor(dst, src, ebl[:, t:t + 1], PS[:D, 6 + t % 2, 0:D],
                                                               ALU.mult, ALU.add).then_inc(c_s.sem, 1)
                            dve.wait_ge(c_o.sem, c_o.at(n))
                            oc = cat[:, :, bass.ds(h * D + col0, D)]
                            nc.vector.tensor_copy(oc[:, 0:NT, :], PS[:, 4, :].rearrange("p (i d) -> p i d", d=D))
                            nc.vector.tensor_copy(oc[:TS, NT, :], PS[:TS, 5, 0:D]).then_inc(c_tail.sem, 1)
                            assert step.n == DSTEPS, step.n
                        in_pairs(dve, 0, HC, head)

                    @block.tensor
                    def _(pe):
                        def head(h, s, k):
                            n = l * HC + h
                            pe.wait_ge(c_in[s].sem, c_in[s].at(l * ((HC + 1 - s) // 2) + k))
                            pe.wait_ge(c_qm.sem, c_qm.at(n))
                            pe.wait_ge(c_km.sem, c_km.at(n))

                            def products(t):
                                q0, w, _ = UNITS[t]
                                pe.wait_ge(c_attc.sem, c_attc.at(n, {0: 0, 1: -1}.get(t, t - 1)))
                                hold(pe)
                                bank = PS[:, t % 2, :]
                                pair = lambda dst, lv, sc, tc, m: nc.tensor.matmul(
                                    dst, kL[:, lv, q0 + sc:q0 + sc + m], qL[:, lv, q0 + tc:q0 + tc + m], start=True, stop=True)
                                if t < NT:
                                    pair(bank[0:64, 0:64], 0, 0, 64, 64)
                                    pair(bank[0:32, 64:96], 1, 0, 32, 32)
                                    pair(bank[64:96, 64:96], 1, 64, 96, 32)
                                for j in range(w // 32):
                                    for z in range(NL):
                                        pair(bank[32 * j:32 * j + 32, 96 + 32 * z:128 + 32 * z], 2 + z, 32 * j, 32 * j, 32)
                                nc.tensor.transpose(PS[:w, 2 + t % 2, 0:D], kd[:, q0:q0 + w], ident[:D, :D]).then_inc(c_att.sem, 1)

                            def outputs(t):
                                q0, w, _ = UNITS[t]
                                pe.wait_ge(c_attd.sem, c_attd.at(n, t + 1))
                                pe.wait_ge(c_attc.sem, c_attc.at(n, t + 1))
                                if t == 0:
                                    pe.wait_ge(c_tail.sem, c_tail.at(n - 1))
                                pe.wait_ge(c_s.sem, c_s.at(n, {0: 0, 1: -1}.get(t, t - 1)))
                                hold(pe)
                                nc.tensor.matmul(PS[:D, 6 + t % 2, 0:D], kdT[:w, t % 2, :], v[:w, s, t, :], start=True, stop=True)\
                                    .then_inc(c_su.sem, 1)
                                if t > 0:
                                    pe.wait_ge(c_s.sem, c_s.at(n, t))
                                    hold(pe)
                                dst = PS[:, 4, t * D:(t + 1) * D] if t < NT else PS[:TS, 5, 0:D]
                                state = st[:, t % 2, :] if t < NT else s0[:, s, :]
                                nc.tensor.matmul(dst, qe[:, q0:q0 + w], state, start=True, stop=False)
                                nc.tensor.matmul(dst, at_[:w, t % 2, 0:w], v[:w, s, t, :], start=False, stop=True)\
                                    .then_inc(c_o.sem, 1)
                            products(0)
                            for t in range(1, NU):
                                products(t)
                                outputs(t - 1)
                            outputs(NU - 1)
                        in_pairs(pe, 0, HC, head)

        def merge(l, cat, catT):
            with ExitStack() as c:
                cg = sb(c, "cg", [P, NU, HC * D])
                sq = sb(c, "msq", [P, NU, HA * D])
                ss = sb(c, "mss", [P, 2, NU, HA])
                groups = ((0, HA, 0, P_AG), (1, HC, HA * D + HB * D, P_CG))
                with nc.Block() as block:
                    @block.sync
                    def _(sp):
                        pn = projN[bass.ds(l, 1), :, C_CG:C_CG + HC * D]
                        sp.dma_start(cg[:, 0:NT, :], pn[:, 0:TP, :].rearrange("a (i p) c -> p (a i) c", p=P)).then_inc(mg_in, 16)
                        sp.dma_start(cg[:TS, NT, :], pn[:, TP:T, :].rearrange("a p c -> p (a c)")).then_inc(mg_in, 16)
                        sp.wait_ge(mg_in, l * 32 + 32)
                        hold(sp)

                    @block.scalar
                    def _(act):
                        for g, nh, c0, pg in groups:
                            if g == 1:
                                act.wait_ge(mg_ss, l * 2 + 1)
                            nc.scalar.activation(sq[:, 0:NT, 0:nh * D], cat[:, 0:NT, c0:c0 + nh * D], ACT.Square)
                            nc.scalar.activation(sq[:TS, NT, 0:nh * D], cat[:TS, NT, c0:c0 + nh * D], ACT.Square).then_inc(mg_sq, 1)
                        act.wait_ge(mg_ss, l * 2 + 2)
                        for g, nh, c0, pg in groups:
                            nc.scalar.activation(ss[:, g, 0:NT, 0:nh], ss[:, g, 0:NT, 0:nh], ACT.Sqrt, bias=epst[:], scale=1.0 / D)
                            nc.scalar.activation(ss[:TS, g, NT, 0:nh], ss[:TS, g, NT, 0:nh], ACT.Sqrt, bias=epst[:TS], scale=1.0 / D)\
                                .then_inc(mg_root, 1)
                        act.wait_ge(mg_in, l * 32 + 32)
                        nc.scalar.activation(cg[:, 0:NT, :], cg[:, 0:NT, :], ACT.Silu)
                        nc.scalar.activation(cg[:TS, NT, :], cg[:TS, NT, :], ACT.Silu).then_inc(mg_silu, 1)
                        for i in range(NU):
                            w = UNITS[i][1]
                            for z in range(2):
                                g = 2 * i + z
                                act.wait_ge(mg_tr.sem, mg_tr.at(l, g + 1))
                                src = PS[:, g % 8, :].rearrange("p (k w) -> p k w", w=P)[:, :, 0:w]
                                nc.scalar.activation(catT[:, 4 * z:4 * z + 4, UNITS[i][0]:UNITS[i][0] + w], src, ACT.Copy)\
                                    .then_inc(mg_ev.sem, 1)

                    @block.vector
                    def _(dve):
                        msteps = 6 + 3 * NU
                        step = Chain(dve, mg_step, l * msteps)
                        for g, nh, c0, pg in groups:
                            dve.wait_ge(mg_sq, l * 2 + g + 1)
                            sqh = sq[:, :, 0:nh * D].rearrange("p i (h d) -> p i h d", d=D)
                            nc.vector.tensor_reduce(ss[:, g, 0:NT, 0:nh], sqh[:, 0:NT], AX, ALU.add)
                            nc.vector.tensor_reduce(ss[:TS, g, NT, 0:nh], sqh[:TS, NT], AX, ALU.add).then_inc(mg_ss, 1)
                        dve.wait_ge(mg_root, l * 2 + 2)
                        for g, nh, c0, pg in groups:
                            step(nc.vector.reciprocal(ss[:, g, 0:NT, 0:nh], ss[:, g, 0:NT, 0:nh]))
                            step(nc.vector.reciprocal(ss[:TS, g, NT, 0:nh], ss[:TS, g, NT, 0:nh]))
                            if g == 0:
                                step(nc.vector.tensor_scalar(ss[:, 0, 0:NT, :], ss[:, 0, 0:NT, :], par[:, P_LI + 1:P_LI + 2], None, ALU.mult))
                                step(nc.vector.tensor_scalar(ss[:TS, 0, NT, :], ss[:TS, 0, NT, :], par[:TS, P_LI + 1:P_LI + 2], None, ALU.mult))
                        dve.wait_ge(mg_silu, l + 1)
                        for g, nh, c0, pg in groups:
                            gain = par[:, pg:pg + D]
                            for i in range(NU):
                                w = UNITS[i][1]
                                o = cat[:w, i, c0:c0 + nh * D].rearrange("p (h d) -> p h d", d=D)
                                step(nc.vector.tensor_tensor(o, o, ss[:w, g, i, 0:nh].unsqueeze(2).to_broadcast([w, nh, D]), ALU.mult))
                                ins = nc.vector.tensor_tensor(o, o, gain[:w].unsqueeze(1).to_broadcast([w, nh, D]), ALU.mult)
                                if g == 1:
                                    step(ins)
                                    ins = nc.vector.tensor_tensor(cat[:w, i, c0:c0 + nh * D], cat[:w, i, c0:c0 + nh * D], cg[:w, i, :], ALU.mult)
                                ins.then_inc(mg_cat, 1)
                        assert step.n == msteps

                    @block.tensor
                    def _(pe):
                        for i in range(NU):
                            q0, w, _ = UNITS[i]
                            pe.wait_ge(mg_cat, l * 2 * NU + NU + i + 1)
                            for z in range(2):
                                g = 2 * i + z
                                if g >= 8:
                                    pe.wait_ge(mg_ev.sem, mg_ev.at(l, g - 7))
                                hold(pe)
                                for kk in range(4):
                                    tr = nc.tensor.transpose(PS[:, g % 8, kk * P:kk * P + w],
                                                             cat[:w, i, (4 * z + kk) * P:(4 * z + kk + 1) * P], ident[:w, :w])
                                tr.then_inc(mg_tr.sem, 1)

        def project_add(l, g, kt, src):
            S = sig_add[g]
            with ExitStack() as c:
                w = sb(c, g, [P, 2, kt, P])
                with nc.Block() as block:
                    @block.sync
                    def _(sp):
                        def load(n, s, k):
                            sp.wait_ge(S["mm"].sem, S["mm"].at(l * KD + n - 2))
                            sp.dma_start(w[:, s, :, :], io[g][bass.ds(l, 1), bass.ds(n, 1)]
                                         .rearrange("a b p (k c) -> p (a b k) c", c=P)).then_inc(S["inn"][s].sem, 16)
                        in_pairs(sp, 0, KD, load)

                    @block.tensor
                    def _(pe):
                        def tile(n, s, k):
                            N = l * KD + n
                            pe.wait_ge(S["inn"][s].sem, S["inn"][s].at(l * (KD // 2) + k))
                            for j in range(NJ):
                                pe.wait_ge(S["add"].sem, S["add"].at(N - 2, j + 1))
                                for kk in range(kt):
                                    mm = nc.tensor.matmul(PS[:, 3 * s + j, 0:JW], w[:, s, kk, :], src[:, kk, cols(j)],
                                                          start=(kk == 0), stop=(kk == kt - 1))
                                mm.then_inc(S["mm"].sem, 1)
                        in_pairs(pe, 0, KD, tile)

                    @block.vector
                    def _(dve):
                        def tile(n, s, k):
                            N = l * KD + n
                            for j in range(NJ):
                                dve.wait_ge(S["mm"].sem, S["mm"].at(N, j + 1))
                                x = xT[:, bass.ds(n, 1), cols(j)].rearrange("p a t -> p (a t)")
                                nc.vector.tensor_tensor(x, PS[:, 3 * s + j, 0:JW], x, ALU.add).then_inc(S["add"].sem, 1)
                        in_pairs(dve, 0, KD, tile)

        def ffn_up(l, xn, hT):
            AW = T + 4
            CVW = AW - 2
            with ExitStack() as c:
                w = sb(c, "uw", [P, 2, 2, KD, P])
                a = sb(c, "ua", [P, 2, AW])
                cv = sb(c, "ucv", [P, 2, CVW])
                cw = sb(c, "ucw", [P, 2, 4])
                tail = sb(c, "utail", [P, NF, 4])
                pieces = {0: [(0, 2, JW)], 1: [(JW, JW + 2, JW)],
                          2: [(2 * JW, 2 * JW + 2, TP - 2 * JW), (TP, TP + 4, TS)]}
                with nc.Block() as block:
                    @block.sync
                    def _(sp):
                        def load(n, s, k):
                            sp.wait_ge(up_g.sem, up_g.at(l * NF + n - 2))
                            sp.dma_start(w[:, s].rearrange("p g k c -> p (g k c)"), io["wu"][bass.ds(l, 1), bass.ds(n, 1)]
                                         .rearrange("a b p c -> p (a b c)")).then_inc(up_in[s].sem, 16)
                        in_pairs(sp, 0, NF, load)
                        sp.wait_ge(up_conv.sem, up_conv.at(l * NF + NF - 1))
                        sp.dma_start(io["tails"][bass.ds(l, 1)].rearrange("a p f c -> p (a f) c"), tail[:]).then_inc(up_tail, 16)
                        sp.wait_ge(up_tail, l * 16 + 16)
                        hold(sp)

                    @block.tensor
                    def _(pe):
                        def tile(n, s, k):
                            N = l * NF + n
                            pe.wait_ge(up_in[s].sem, up_in[s].at(l * (NF // 2) + k))
                            for gate, mmsig, freed in ((0, up_a, up_ev), (1, up_g, up_mul)):
                                for j in range(NJ):
                                    pe.wait_ge(freed.sem, freed.at(N - 1, j + 1))
                                    for kk in range(KD):
                                        mm = nc.tensor.matmul(PS[:, 3 * gate + j, 0:JW], w[:, s, gate, kk, :], xn[:, kk, cols(j)],
                                                              start=(kk == 0), stop=(kk == KD - 1))
                                    mm.then_inc(mmsig.sem, 1)
                        in_pairs(pe, 0, NF, tile)

                    @block.scalar
                    def _(act):
                        def tile(n, s, k):
                            N = l * NF + n
                            act.wait_ge(up_conv.sem, up_conv.at(N - 2))
                            for j in range(NJ):
                                act.wait_ge(up_a.sem, up_a.at(N, j + 1))
                                for t0, a0, wd in pieces[j]:
                                    ins = nc.scalar.activation(a[:, s, a0:a0 + wd], PS[:, j, t0 - j * JW:t0 - j * JW + wd], ACT.Copy)
                                ins.then_inc(up_ev.sem, 1)
                            act.wait_ge(up_conv.sem, up_conv.at(N))
                            nc.scalar.activation(cv[:, s, :], cv[:, s, :], ACT.Silu).then_inc(up_silu.sem, 1)
                        in_pairs(act, 0, NF, tile)

                    @block.vector
                    def _(dve):
                        for s in range(2):
                            z = nc.vector.memset(a[:, s, 0:2], 0.0)
                        z.then_inc(up_zero, 1)
                        dve.wait_ge(up_zero, l + 1)

                        def tile(n, s, k):
                            N = l * NF + n
                            step = Chain(dve, up_step, N * 3)
                            nc.vector.tensor_copy(cw[:, s, :], par[:, bass.ds(n * 4 + P_CONV, 4)])
                            step(nc.vector.tensor_copy(a[:, s, TP + 2:TP + 4], par[:, bass.ds(n * 2 + P_HIST, 2)]))
                            dve.wait_ge(up_ev.sem, up_ev.at(N))
                            nc.vector.tensor_copy(tail[:, bass.ds(n, 1), 0:2].rearrange("p a c -> p (a c)"), a[:, s, TP:TP + 2])
                            nc.vector.tensor_copy(tail[:, bass.ds(n, 1), 2:4].rearrange("p a c -> p (a c)"), a[:, s, AW - 2:AW])
                            step(nc.vector.tensor_scalar(cv[:, s, :], a[:, s, 2:AW], cw[:, s, 2:3], cw[:, s, 3:4], ALU.mult, ALU.add))
                            step(nc.vector.scalar_tensor_tensor(cv[:, s, :], a[:, s, 1:AW - 1], cw[:, s, 1:2], cv[:, s, :],
                                                                ALU.mult, ALU.add))
                            nc.vector.scalar_tensor_tensor(cv[:, s, :], a[:, s, 0:AW - 2], cw[:, s, 0:1], cv[:, s, :],
                                                           ALU.mult, ALU.add).then_inc(up_conv.sem, 1)
                            dve.wait_ge(up_silu.sem, up_silu.at(N))
                            for j in range(NJ):
                                dve.wait_ge(up_g.sem, up_g.at(N, j + 1))
                                for t0, a0, wd in pieces[j]:
                                    ins = nc.vector.tensor_tensor(hT[:, bass.ds(n, 1), t0:t0 + wd].rearrange("p a t -> p (a t)"),
                                                                  PS[:, 3 + j, t0 - j * JW:t0 - j * JW + wd],
                                                                  cv[:, s, a0 - 2:a0 - 2 + wd], ALU.mult)
                                ins.then_inc(up_mul.sem, 1)
                        in_pairs(dve, 0, NF, tile)

        with nc.Fori(0, L) as l:
            load_params(l)
            with ExitStack() as c:
                xn = sb(c, "xn", [P, KD, T])
                rms_norm(l * 2, par[:, P_N1:P_N1 + KD], xn)
                project_features(l, xn)
                project_tokens(l, xn)
            with ExitStack() as c:
                cat = sb(c, "cat", [P, NU, DM])
                with ExitStack() as cb_:
                    bias = sb(cb_, "bias", [P, NBIAS])
                    index_scores(l, bias)
                    attention(l, "b", HB, 1, cat, HA * D, bias)
                attention(l, "a", HA, 2, cat, 0)
                hgrn(l, cat, (HA + HB) * D)
                catT = sb(c, "catT", [P, KD, T])
                merge(l, cat, catT)
                project_add(l, "wo", KD, catT)
            with ExitStack() as c:
                hT = sb(c, "hT", [P, NF, T])
                with ExitStack() as c2:
                    xn = sb(c2, "xn2", [P, KD, T])
                    rms_norm(l * 2 + 1, par[:, P_N2:P_N2 + KD], xn)
                    ffn_up(l, xn, hT)
                project_add(l, "wd", NF, hT)

        yT = sb(ctx, "yT", [P, KD, T])
        rms_norm(2 * L, fgain, yT)
        with nc.Block() as block:
            @block.sync
            def _(sp):
                sp.dma_start(io["yT"].rearrange("(k p) t -> p k t", p=P), yT[:]).then_inc(s_yout, 16)
                sp.wait_ge(s_yout, 16)


def kernel(**inputs):
    import math
    import numpy as np
    import concourse.bacc as bacc
    from concourse.bass_utils import run_bass_kernel_spmd

    a = {k: np.asarray(v) for k, v in inputs.items()}
    nc = bacc.Bacc("TRN2", target_bir_lowering=False, num_devices=1)

    names = ["aq", "ak", "av", "bq", "bk", "bv", "iq", "ik", "iw", "cq", "cf", "ci", "cg"]
    sizes = [384, 384, 384, 320, 320, 320, 256, 64, 4, 320, 320, 320, 320]
    off = np.concatenate([[0], np.cumsum(sizes)])
    col = {nm: np.arange(off[i], off[i + 1]) for i, nm in enumerate(names)}
    w_in = a["w_in"]
    wf = w_in[:, :, np.concatenate([col[x] for x in ("aq", "ak", "iq", "ik", "bq", "bk", "cq", "cf")])]
    wf = np.concatenate([wf, np.zeros((L, DM, NPT * P - wf.shape[2]), np.float32)], axis=2)
    wn = w_in[:, :, np.concatenate([col[x] for x in ("av", "bv", "iw", "ci", "cg")])]

    def tiles(w, width):
        l_, k_, n_ = w.shape
        return w.reshape(l_, k_ // P, P, n_ // width, width).transpose(0, 3, 2, 1, 4).reshape(l_, n_ // width, P, -1)

    up = tiles(a["ffn_up"], P)
    wu = np.stack([up[:, :NF], up[:, NF:]], axis=3)

    pos = np.concatenate([np.arange(TP), PAST + np.arange(TS)]).astype(np.float32)

    def table(width):
        inv = (10000.0 ** (-np.arange(0, width, 2, dtype=np.float32).astype(np.float64) / width)).astype(np.float32)
        ang = (pos[None, :] * inv[:, None]).astype(np.float32).astype(np.float64)
        cos = np.concatenate([np.cos(ang), np.cos(ang)])
        sin = np.concatenate([-np.sin(ang), np.sin(ang)])
        return [np.tile(x, (P // width, 1)).astype(np.float32) for x in (cos, sin)]

    def swap(width):
        p = np.arange(P)
        m = np.zeros((P, P), np.float32)
        m[p, p // width * width + (p % width + width // 2) % width] = 1
        return m

    s_, t_ = np.arange(32)[:, None], np.arange(32)[None, :]
    lm = [((s_ // (2 * h) == t_ // (2 * h)) & (s_ % (2 * h) < h) & (t_ % (2 * h) >= h)) for h in (16, 8, 4, 2)]
    lm.append((s_ // 2 == t_ // 2) & (s_ <= t_))
    lmask = np.tile(np.stack(lm, axis=1), (4, 1, 1)).astype(np.float32)
    bmask = np.repeat((np.arange(P)[:, None] // 32 == np.arange(4)[None, :])[:, :, None], 32, axis=2).astype(np.float32)

    def per_feature(x, k):
        return x.reshape(L, k, P).transpose(0, 2, 1)

    conv = np.concatenate([a["ffn_conv_w"], a["ffn_conv_b"][:, None]], axis=1)
    conv = conv.reshape(L, 4, NF, P).transpose(0, 3, 2, 1).reshape(L, P, NF * 4)
    hist = a["state_ffn_conv"][:, 0].reshape(L, 2, NF, P).transpose(0, 3, 2, 1).reshape(L, P, NF * 2)
    wide = lambda x: np.broadcast_to(x[:, None, :], (L, P, x.shape[1]))
    li = np.array([[0.8 - 0.6 * math.exp(-0.3 * i), 1.0 - (0.8 - 0.6 * math.exp(-0.3 * i))] for i in range(L)], np.float32)
    params = np.concatenate([
        per_feature(a["norm1"], KD), per_feature(a["norm2"], KD), conv, hist, wide(a["a_norm"]), wide(a["c_norm"]),
        wide(a["lam_q1"]), wide(a["lam_k1"]), wide(a["lam_q2"]), wide(a["lam_k2"]), wide(li)], axis=2)

    arrays = {
        "xT": np.concatenate([a["x_prompt"][0], a["x_sample"][0]]).T,
        "wf": tiles(wf, P), "wn": tiles(wn, CW), "wo": tiles(a["w_out"], P), "wu": wu.reshape(L, NF, P, -1),
        "wd": tiles(a["ffn_down"], P), "rope": np.stack(table(32) + table(64)), "swapA": swap(32), "swapB": swap(64),
        "ident": np.eye(P, dtype=np.float32), "ones": np.ones((P, P), np.float32), "lmask": lmask, "bmask": bmask,
        "fgain": a["final_norm"].reshape(KD, P).T, "clow": a["c_lower"].reshape(L, HC, D).transpose(2, 0, 1),
        "params": params, "kidx": a["cache_b_kidx"][:, 0].transpose(0, 2, 1), "s0": a["state_c"][:, 0],
        "ak": a["cache_a_k"][:, 0].transpose(0, 2, 3, 1), "bk": a["cache_b_k"][:, 0].transpose(0, 2, 3, 1),
        "av": a["cache_a_v"][:, 0].reshape(L, PAST // P, P, HA, D).transpose(0, 3, 2, 1, 4),
        "bv": a["cache_b_v"][:, 0].reshape(L, PAST // P, P, HB, D).transpose(0, 3, 2, 1, 4),
    }
    outs = {"yT": (DM, T), "projT": (L, NPT * P, T), "projN": (L, T, WN), "stateC": (L, HC, D, 2, D), "tails": (L, P, NF, 4)}
    arrays = {"in_" + k: np.ascontiguousarray(v) for k, v in arrays.items()}
    io = {k[3:]: nc.dram_tensor(k, v.shape, F32, kind="ExternalInput").ap() for k, v in arrays.items()}
    io.update({k: nc.dram_tensor("out_" + k, v, F32, kind="ExternalOutput").ap() for k, v in outs.items()})
    build(nc, io)
    r = run_bass_kernel_spmd(nc, [arrays], core_ids=[0]).results[0]
    y, pT, pN, sC, tl = (np.asarray(r["out_" + k]) for k in outs)

    def group(t0, t1, m):
        rows = lambda r0, h: pT[:, r0:r0 + h * D, t0:t1].reshape(L, h, D, t1 - t0).transpose(0, 3, 1, 2)[:, None]
        vals = lambda c0, h: pN[:, t0:t1, c0:c0 + h * D].reshape(L, 1, t1 - t0, h, D)
        tail = tl[:, :, :, 2 * m:2 * m + 2].transpose(0, 3, 2, 1).reshape(L, 1, 2, DFF)
        return (rows(R_AK, HA), vals(C_AV, HA), rows(R_BK, HB), vals(C_BV, HB), rows(R_IK, 1)[:, :, :, 0],
                sC[:, None, :, :, m], tail)
    return (y[:, :TP].T[None], y[:, TP:].T[None]) + group(0, TP, 0) + group(TP, T, 1)
```

```python
import concourse.bass as bass
from concourse import mybir
from contextlib import ExitStack

F32 = mybir.dt.float32
ALU = mybir.AluOpType
ACT = mybir.ActivationFunctionType
AX = mybir.AxisListType.X

P = 128
L, DM, TP, TS, PAST = 2, 1024, 1024, 32, 512
T = TP + TS
NJ, JW = 3, 352
KD = DM // P
HA, HB, HC, HI, D = 6, 5, 5, 4, 64
DFF = 2816
NF = DFF // P
NT = TP // P
EPS = 1e-6
NEG = -1e30
SENTINEL = -3e38
TOP_P, TOP_S = 256, (PAST + TS) // 4
R_IQ, R_IK, R_BQ, R_BK, R_CQ, R_CF, R_AQ, R_AK = 0, 256, 320, 640, 960, 1280, 1664, 2048
NPT = 19
LEAD = (0, 1, 2)
ROTATED = {n: (0 if n >= 13 else 2, 64 if n == 7 else P) for n in (*range(8), *range(13, NPT))}
C_AV, C_BV, C_CI, C_CG, WN = 0, 384, 704, 1024, 1344
NC4, CW = 4, WN // 4
P_N1, P_N2, P_CONV, P_HIST, P_AG, P_CG, P_LAM, P_LI, PCOLS = 0, 8, 16, 104, 148, 212, 276, 404, 406
UNITS = [(i * P, P, (i + 1) * P) for i in range(NT)] + [(TP, TS, PAST + TS)]
NU = len(UNITS)
KEY0 = [0] * NT + [TP]
VT0 = [0] * NT + [NT]
GROUPS = [[list(range(a, min(a + 4, -(-nk // P)))) for a in range(0, -(-nk // P), 4)] for _, _, nk in UNITS]
GEND = [sum(len(g) for g in GROUPS[:i + 1]) for i in range(NU)]
NG = GEND[-1]
BOFF = [sum(u[2] for u in UNITS[:i]) for i in range(NU)]
NBIAS = sum(u[2] for u in UNITS)
HALVES = (64, 32, 16, 8, 4, 2)
NL = 5


def cols(j):
    return slice(j * JW, (j + 1) * JW)


class Signal:

    every = []

    def __init__(self, ctx, nc, name, per=1):
        self.sem, self.per = ctx.enter_context(nc.semaphore(name)), per
        Signal.every.append(self)

    def at(self, n, k=None):
        return (n + 3) * self.per if k is None else (n + 2) * self.per + k


class Chain:

    def __init__(self, eng, sem, base=0):
        self.eng, self.sem, self.base, self.n = eng, sem, base, 0

    def __call__(self, ins):
        self.n += 1
        ins.then_inc(self.sem, 1)
        self.eng.wait_ge(self.sem, self.base + self.n)


HOLD = []


def hold(eng):
    eng.sem_inc(HOLD[0], 1)


def in_pairs(eng, lo, hi, body):
    pairs = (hi - lo) // 2
    if pairs:
        hold(eng)
        with eng.Fori(0, pairs) as it:
            for s in range(2):
                body(2 * it + (lo + s), s, it + lo // 2)
    if (hi - lo) % 2:
        body(hi - 1, (hi - 1) % 2, (hi - 1) // 2)
    hold(eng)


def build(nc, io):
    ctx = ExitStack()
    Signal.every = []
    with ctx:
        made = []

        def sb(c, name, shape):
            made.append(name)
            again = made.count(name) - 1
            return c.enter_context(nc.sbuf_tensor(name + str(again) * bool(again), shape, F32))

        def sem(name):
            return ctx.enter_context(nc.semaphore(name))

        def sig(name, per=1):
            return Signal(ctx, nc, name, per)

        ident = sb(ctx, "ident", [P, P])
        ones = sb(ctx, "ones", [P, P])
        swapA = sb(ctx, "swapA", [P, P])
        swapB = sb(ctx, "swapB", [P, P])
        lmask = sb(ctx, "lmask", [P, NL, 32])
        bmask = sb(ctx, "bmask", [P, 4, 32])
        epst = sb(ctx, "epst", [P, 1])
        fgain = sb(ctx, "fgain", [P, KD])
        clow = sb(ctx, "clow", [D, L, HC])
        lower = sb(ctx, "lower", [D, L, HC])
        lbf = sb(ctx, "lbf", [D, L, HC])
        omlb = sb(ctx, "omlb", [D, L, HC])
        par = sb(ctx, "par", [P, PCOLS])
        neglam = sb(ctx, "neglam", [P, 1])
        xT = sb(ctx, "xT", [P, KD, T])
        PS = ctx.enter_context(nc.psum_tensor("PS", [P, 8, 512], F32))
        projT, projN = io["projT"], io["projN"]

        s_const, s_x = sem("s_const"), sem("s_x")
        HOLD[:] = [sem("waits_passed")]
        s_chain_setup, s_lowexp = sem("s_chain_setup"), sem("s_lowexp")
        s_par, s_lam, s_lamexp, s_chain_lam = sem("s_par"), sem("s_lam"), sem("s_lamexp"), sem("s_chain_lam")

        norm_sq, norm_used, norm_sum = sig("norm_sq", 8), sig("norm_used", 8), sig("norm_sum", 3)
        norm_root, norm_inv, norm_step = sig("norm_root"), sig("norm_inv"), sem("norm_step")
        proj = {}
        for g, nt, nc_ in (("lead", len(LEAD), 0), ("rest", NPT - len(LEAD), NC4)):
            nr = len(LEAD) if g == "lead" else len(ROTATED) - len(LEAD)
            nl = nt + nc_
            proj[g] = dict(
                inn=[sig(f"{g}_in0", 16 * ((nl + 1) // 2)), sig(f"{g}_in1", 16 * (nl // 2))], rope=sem(f"{g}_rope"),
                mm=sig(f"{g}_mm", 3 * nt), ev=sig(f"{g}_ev", 3 * nt), swap=sig(f"{g}_swap", 3 * nr),
                swapped=sig(f"{g}_swapped", 3 * nr), prod=sig(f"{g}_prod", 2 * nr), sum=sig(f"{g}_sum", nr),
                out=[sig(f"{g}_out0", 16 * ((nt + 1) // 2)), sig(f"{g}_out1", 16 * (nt // 2))],
                tmm=sig(f"{g}_tmm", NU * NC4), tev=sig(f"{g}_tev", NU * NC4), tout=sig(f"{g}_tout", 32 * NC4))
        iw_in, iw_mm, iw_ev = sem("iw_in"), sem("iw_mm"), sem("iw_ev")
        ix_in, ix_dots, ix_relu, ix_acc = sem("ix_in"), sig("ix_dots", 28), sig("ix_relu", 28), sig("ix_acc", 28)
        ix_step, ix_pick = sem("ix_step"), sem("ix_pick")
        att = {}
        for g, maps in (("a", 2), ("b", 1)):
            att[g] = dict(
                inn=[sig(f"{g}_in0", 16 * 7), sig(f"{g}_in1", 16 * 7)], scores=sig(f"{g}_scores", NU * maps),
                negmax=sig(f"{g}_negmax", NU * maps), exp=sig(f"{g}_exp", NU * maps),
                comb=sig(f"{g}_comb", NU), tr=sig(f"{g}_tr", NG), ptc=sig(f"{g}_ptc", NG),
                pv=sig(f"{g}_pv", NU), inv=sig(f"{g}_inv", NU), out=sig(f"{g}_out", NU), step=sem(f"{g}_step"))
        c_in = [sig("c_in0", 16 * 5), sig("c_in1", 16 * 5)]
        c_gate, c_inv, c_q, c_x, c_ln = sig("c_gate", 2), sig("c_inv"), sig("c_q"), sig("c_x"), sig("c_ln")
        c_d, c_e, c_qm, c_km, c_last = sig("c_d", 10), sig("c_e", 10), sig("c_qm", 8), sig("c_km", 8), sig("c_last")
        c_att, c_attd, c_attc = sig("c_att", NU), sig("c_attd", NU), sig("c_attc", NU)
        c_o, c_su, c_s, c_tail = sig("c_o", NU), sig("c_su", NU), sig("c_s", NU), sig("c_tail")
        c_out = [sig("c_out0", 16), sig("c_out1", 16)]
        c_abs, c_dstep = sem("c_abs"), sem("c_dstep")
        mg_in, mg_sq, mg_ss, mg_root, mg_silu = sem("mg_in"), sem("mg_sq"), sem("mg_ss"), sem("mg_root"), sem("mg_silu")
        mg_step, mg_cat, mg_tr, mg_ev = sem("mg_step"), sem("mg_cat"), sig("mg_tr", 18), sig("mg_ev", 18)
        sig_add = {}
        for g in ("wo", "wd"):
            sig_add[g] = dict(inn=[sig(f"{g}_in0", 16), sig(f"{g}_in1", 16)], mm=sig(f"{g}_mm", 3), add=sig(f"{g}_add", 3))
        up_in = [sig("up_in0", 16), sig("up_in1", 16)]
        up_a, up_g, up_ev, up_conv = sig("up_a", 3), sig("up_g", 3), sig("up_ev", 3), sig("up_conv")
        up_silu, up_mul, up_step, up_zero = sig("up_silu"), sig("up_mul", 3), sem("up_step"), sem("up_zero")
        up_tail = sem("up_tail")
        s_y, s_yout = sem("s_y"), sem("s_yout")

        with nc.Block() as block:
            consts = [(ident, "ident"), (ones, "ones"), (swapA, "swapA"), (swapB, "swapB"), (lmask, "lmask"),
                      (bmask, "bmask"), (fgain, "fgain"), (clow, "clow")]

            @block.sync
            def _(sp):
                for t, name in consts:
                    sp.dma_start(t[:], io[name]).then_inc(s_const, 16)
                for k in range(KD):
                    sp.dma_start(xT[:, k, :], io["xT"][k * P:(k + 1) * P, :]).then_inc(s_x, 16)
                sp.wait_ge(s_const, 16 * len(consts))
                sp.wait_ge(s_x, 16 * KD)

            @block.gpsimd
            def _(pool):
                for s in Signal.every:
                    pool.sem_inc(s.sem, 2 * s.per)

            @block.scalar
            def _(act):
                act.wait_ge(s_chain_setup, 3)
                nc.scalar.activation(lower[:], lower[:], ACT.Exp).then_inc(s_lowexp, 1)

            @block.vector
            def _(dve):
                step = Chain(dve, s_chain_setup)
                step(nc.vector.memset(epst[:], EPS))
                dve.wait_ge(s_const, 16 * len(consts))
                mx, sm = omlb[:, 0, :], omlb[:, 1, :]
                step(nc.vector.tensor_tensor(mx, clow[:, 0, :], clow[:, 1, :], ALU.max))
                step(nc.vector.tensor_tensor(lower[:], clow[:], mx.unsqueeze(1).to_broadcast([D, L, HC]), ALU.subtract))
                dve.wait_ge(s_lowexp, 1)
                step(nc.vector.tensor_tensor(sm, lower[:, 0, :], lower[:, 1, :], ALU.add))
                step(nc.vector.reciprocal(mx, sm))
                step(nc.vector.tensor_tensor(lbf[:], lower[:], mx.unsqueeze(1).to_broadcast([D, L, HC]), ALU.mult))
                step(nc.vector.tensor_tensor(lower[:, 0, :], lbf[:, 0, :], lbf[:, 0, :], ALU.subtract))
                step(nc.vector.tensor_tensor(sm, lbf[:, 0, :], lbf[:, 1, :], ALU.add))
                step(nc.vector.tensor_tensor(lower[:, 1, :], sm, lbf[:, 0, :], ALU.subtract))
                step(nc.vector.tensor_scalar(omlb[:], lower[:], -1.0, 1.0, ALU.mult, ALU.add))
                step(nc.vector.tensor_scalar(lbf[:], lower[:], 1e-20, None, ALU.max))

        def rms_norm(n, gain, dst, extra=None):
            with ExitStack() as c:
                sq = sb(c, "sq", [P, 2, T])
                inv = sb(c, "inv", [P, T])
                with nc.Block() as block:
                    @block.scalar
                    def _(act):
                        for k in range(KD):
                            act.wait_ge(norm_used.sem, norm_used.at(n, k - 1))
                            nc.scalar.activation(sq[:, k % 2, :], xT[:, k, :], ACT.Square).then_inc(norm_sq.sem, 1)
                        act.wait_ge(norm_sum.sem, norm_sum.at(n))
                        nc.scalar.activation(inv[:].rearrange("p (j w) -> p j w", j=NJ), PS[:, 0:NJ, 0:JW], ACT.Sqrt,
                                             bias=epst[:], scale=1.0 / DM).then_inc(norm_root.sem, 1)

                    @block.tensor
                    def _(pe):
                        for k in range(KD):
                            pe.wait_ge(norm_sq.sem, norm_sq.at(n, k + 1))
                            for j in range(NJ):
                                mm = nc.tensor.matmul(PS[:, j, 0:JW], ones[:], sq[:, k % 2, cols(j)],
                                                      start=(k == 0), stop=(k == KD - 1))
                                if k == KD - 1:
                                    mm.then_inc(norm_sum.sem, 1)
                            if k < KD - 1:
                                mm.then_inc(norm_used.sem, 1)
                        pe.sem_inc(norm_used.sem, 1)

                    @block.vector
                    def _(dve):
                        dve.wait_ge(norm_root.sem, norm_root.at(n))
                        nc.vector.reciprocal(inv[:], inv[:]).then_inc(norm_inv.sem, 1)
                        dve.wait_ge(norm_inv.sem, norm_inv.at(n))
                        for k in range(KD):
                            nc.vector.scalar_tensor_tensor(dst[:, k, :], xT[:, k, :], gain[:, k:k + 1], inv[:],
                                                           ALU.mult, ALU.mult).then_inc(norm_step, 1)
                    if extra:
                        extra(block)

        def load_params(l):
            with nc.Block() as block:
                @block.sync
                def _(sp):
                    sp.dma_start(par[:], io["params"][bass.ds(l, 1)].rearrange("o p c -> p (o c)")).then_inc(s_par, 16)
                    sp.wait_ge(s_par, l * 16 + 16)
                    hold(sp)

                @block.scalar
                def _(act):
                    act.wait_ge(s_lam, l + 1)
                    nc.scalar.activation(par[:, P_LAM:P_LAM + 2], par[:, P_LAM:P_LAM + 2], ACT.Exp).then_inc(s_lamexp, 1)

                @block.vector
                def _(dve):
                    step = Chain(dve, s_chain_lam, l * 4)
                    dve.wait_ge(s_par, l * 16 + 16)
                    lam = par[:, P_LAM:P_LAM + 128].rearrange("p (m w d) -> p m w d", m=2, w=2)
                    prod = par[:, P_LAM + 64:P_LAM + 128].rearrange("p (m d) -> p m d", m=2)
                    step(nc.vector.tensor_tensor(par[:, P_LAM:P_LAM + 32], lam[:, 0, 0, :], lam[:, 0, 1, :], ALU.mult))
                    step(nc.vector.tensor_tensor(par[:, P_LAM + 32:P_LAM + 64], lam[:, 1, 0, :], lam[:, 1, 1, :], ALU.mult))
                    both = par[:, P_LAM:P_LAM + 64].rearrange("p (m d) -> p m d", m=2)
                    step(nc.vector.tensor_reduce(prod[:, 0, 0:2], both, AX, ALU.add))
                    nc.vector.tensor_copy(par[:, P_LAM:P_LAM + 2], prod[:, 0, 0:2]).then_inc(s_lam, 1)
                    dve.wait_ge(s_lamexp, l + 1)
                    step(nc.vector.tensor_tensor(neglam[:], par[:, P_LAM + 1:P_LAM + 2], par[:, P_LAM:P_LAM + 1], ALU.subtract))
                    nc.vector.tensor_tensor(neglam[:], neglam[:], par[:, P_LI:P_LI + 1], ALU.subtract)

        def project(l, g, xn, iw, bias=None):
            S = proj[g]
            tiles = LEAD if g == "lead" else tuple(range(len(LEAD), NPT))
            chunks = 0 if g == "lead" else NC4
            nt = len(tiles)
            rot = {n: i for i, n in enumerate(n for n in tiles if n in ROTATED)}
            units = list(range(2, NU)) if g == "rest" else []
            rounds = [TOP_P // 8] * (len(units) - 1) + [TOP_S // 8]
            dots_at = dict(zip((0, 1, 3, 6, 9, 13, 24), range(len(units))))
            with ExitStack() as c:
                w = sb(c, "pw", [P, 2, KD * max(P, CW)])
                u = sb(c, "pu", [P, 2, T])
                us = sb(c, "pus", [P, 2, T])
                cosb = sb(c, "pcosb", [P, T])
                tab = sb(c, "ptab", [P, 4, T])
                if g == "lead":
                    wiw = sb(c, "wiw", [P, KD, HI])
                else:
                    tout = sb(c, "ptout", [P, NU, CW])
                    iq = sb(c, "iq", [D, HI, T])
                    ik = sb(c, "ik", [D, T + PAST])
                    rl = sb(c, "rl", [P, HI, TP])
                    work = sb(c, "work", [P, TP])
                    top = sb(c, "top", [P, 8])
                wf = lambda q: w[:, q % 2, 0:KD * P].rearrange("p (k c) -> p k c", c=P)
                wn = lambda q: w[:, q % 2, 0:KD * CW].rearrange("p (k c) -> p k c", c=CW)
                nload = 4
                with nc.Block() as block:
                    @block.sync
                    def _(sp):
                        if units:
                            pt = projT[bass.ds(l, 1)]
                            for dst, src in (
                                    (iq[:], pt[:, R_IQ:R_IQ + HI * D, :].rearrange("a (h p) t -> p (a h) t", p=D)),
                                    (ik[:, 0:TP], pt[:, R_IK:R_IK + D, 0:TP].rearrange("a p t -> p (a t)")),
                                    (ik[:, TP + PAST:], pt[:, R_IK:R_IK + D, TP:T].rearrange("a p t -> p (a t)")),
                                    (ik[:, TP:TP + PAST], io["kidx"][bass.ds(l, 1)].rearrange("a p t -> p (a t)"))):
                                sp.dma_start(dst, src).then_inc(ix_in, 16)
                        else:
                            sp.dma_start(wiw[:], io["wiw"][bass.ds(l, 1)].rearrange("a p k c -> p (a k) c")).then_inc(iw_in, 16)

                        def load(q):
                            if q < nt:
                                if q >= 2:
                                    sp.wait_ge(S["mm"].sem, S["mm"].at(l, 3 * (q - 1)))
                                    hold(sp)
                                sp.dma_start(wf(q), io["wf"][bass.ds(l, 1), tiles[q]].rearrange("a p (k c) -> p (a k) c", c=P))\
                                    .then_inc(S["inn"][q % 2].sem, 16)
                            else:
                                if q - 2 < nt:
                                    sp.wait_ge(S["mm"].sem, S["mm"].at(l, 3 * (q - 1)))
                                else:
                                    sp.wait_ge(S["tmm"].sem, S["tmm"].at(l, NU * (q - 1 - nt)))
                                hold(sp)
                                sp.dma_start(wn(q), io["wn"][bass.ds(l, 1), q - nt].rearrange("a p (k c) -> p (a k) c", c=CW))\
                                    .then_inc(S["inn"][q % 2].sem, 16)

                        def store(q):
                            n = tiles[q]
                            if n in rot:
                                sp.wait_ge(S["sum"].sem, S["sum"].at(l, rot[n] + 1))
                            else:
                                sp.wait_ge(S["ev"].sem, S["ev"].at(l, 3 * q + 3))
                            hold(sp)
                            sp.dma_start(projT[bass.ds(l, 1), n * P:(n + 1) * P].rearrange("a p t -> p (a t)"),
                                         (us if n in rot else u)[:, q % 2, :]).then_inc(S["out"][q % 2].sem, 16)

                        def store_chunk(k):
                            sp.wait_ge(S["tev"].sem, S["tev"].at(l, NU * (k + 1)))
                            hold(sp)
                            rows = projN[bass.ds(l, 1), :, k * CW:(k + 1) * CW]
                            sp.dma_start(rows[:, 0:TP, :].rearrange("a (i p) c -> p (a i) c", p=P), tout[:, 0:NT, :])\
                                .then_inc(S["tout"].sem, 16)
                            sp.dma_start(rows[:, TP:T, :].rearrange("a p c -> p (a c)"), tout[:TS, NT, :])\
                                .then_inc(S["tout"].sem, 16)
                        load(0)
                        sp.dma_start(tab[:, 2:4, :], io["rope"][2:4].rearrange("h p t -> p h t")).then_inc(S["rope"], 16)
                        load(1)
                        sp.dma_start(tab[:, 0:2, :], io["rope"][0:2].rearrange("h p t -> p h t")).then_inc(S["rope"], 16)
                        for q in range(2, nt + chunks + 2):
                            if q < nt + chunks:
                                load(q)
                            if q - 2 < nt:
                                store(q - 2)
                            else:
                                store_chunk(q - 2 - nt)
                        for x in range(2):
                            sp.wait_ge(S["out"][x].sem, S["out"][x].at(l))
                            hold(sp)
                        if chunks:
                            sp.wait_ge(S["tout"].sem, S["tout"].at(l))
                        hold(sp)

                    @block.tensor
                    def _(pe):
                        def loaded(q):
                            pe.wait_ge(S["inn"][q % 2].sem, S["inn"][q % 2].at(l, 16 * (q // 2 + 1)))

                        def swap(r):
                            n = list(rot)[r // 3]
                            q, j = tiles.index(n), r % 3
                            pe.wait_ge(S["ev"].sem, S["ev"].at(l, 3 * q + j + 1))
                            if r:
                                pe.wait_ge(S["swapped"].sem, S["swapped"].at(l, r))
                            nc.tensor.matmul(PS[:, 3, 0:JW], (swapA if ROTATED[n][0] == 0 else swapB)[:], u[:, q % 2, cols(j)],
                                             start=True, stop=True).then_inc(S["swap"].sem, 1)

                        def dots(y):
                            i = units[y]
                            q0, nq, nk = UNITS[i]
                            pe.wait_ge(ix_in, (l + 1) * 16 * nload)
                            for h in range(HI):
                                pe.wait_ge(ix_relu.sem, ix_relu.at(l, HI * y + h - 1))
                                hold(pe)
                                for a in range(0, nk, 512):
                                    b = min(nk, a + 512)
                                    mm = nc.tensor.matmul(PS[:nq, 4 + 2 * (h % 2) + a // 512, 0:b - a], iq[:, h, q0:q0 + nq],
                                                          ik[:, KEY0[i] + a:KEY0[i] + b], start=True, stop=True)
                                mm.then_inc(ix_dots.sem, 1)
                        r = 0
                        for q in range(nt):
                            if q in dots_at and units:
                                dots(dots_at[q])
                            loaded(q)
                            for j in range(NJ):
                                if q:
                                    pe.wait_ge(S["ev"].sem, S["ev"].at(l, 3 * q + j - 2))
                                for kk in range(KD):
                                    mm = nc.tensor.matmul(PS[:, j, 0:JW], wf(q)[:, kk, :], xn[:, kk, cols(j)],
                                                          start=(kk == 0), stop=(kk == KD - 1))
                                mm.then_inc(S["mm"].sem, 1)
                                if r < 3 * len(rot) and (tiles.index(list(rot)[r // 3]), r % 3) < (q, j):
                                    swap(r)
                                    r += 1
                        while r < 3 * len(rot):
                            swap(r)
                            r += 1
                        for x in range(chunks * NU):
                            k, i = divmod(x, NU)
                            q0, nq, _ = UNITS[i]
                            if nt + x in dots_at:
                                dots(dots_at[nt + x])
                            if i == 0:
                                loaded(nt + k)
                            pe.wait_ge(S["tev"].sem, S["tev"].at(l, x - 2)) if x > 2 else pe.wait_ge(S["ev"].sem, S["ev"].at(l))
                            for kk in range(KD):
                                mm = nc.tensor.matmul(PS[:nq, x % 3, 0:CW], xn[:, kk, q0:q0 + nq], wn(nt + k)[:, kk, :],
                                                      start=(kk == 0), stop=(kk == KD - 1))
                            mm.then_inc(S["tmm"].sem, 1)
                        if g == "lead":
                            pe.wait_ge(iw_in, l * 16 + 16)
                            for i, (q0, nq, _) in enumerate(UNITS):
                                for kk in range(KD):
                                    mm = nc.tensor.matmul(PS[:nq, 7, i * HI:(i + 1) * HI], xn[:, kk, q0:q0 + nq], wiw[:, kk, :],
                                                          start=(kk == 0), stop=(kk == KD - 1))
                            mm.then_inc(iw_mm, 1)

                    @block.scalar
                    def _(act):
                        def swapped(r):
                            n = list(rot)[r // 3]
                            q, j = tiles.index(n), r % 3
                            act.wait_ge(S["swap"].sem, S["swap"].at(l, r + 1))
                            nc.scalar.activation(us[:, q % 2, cols(j)], PS[:, 3, 0:JW], ACT.Copy).then_inc(S["swapped"].sem, 1)

                        def relu(y):
                            i = units[y]
                            q0, nq, nk = UNITS[i]
                            for h in range(HI):
                                act.wait_ge(ix_dots.sem, ix_dots.at(l, HI * y + h + 1))
                                act.wait_ge(ix_acc.sem, ix_acc.at(l, HI * (y - 1) + h + 1))
                                b = 4 + 2 * (h % 2)
                                src = PS[:nq, b:b + 2, :].rearrange("p b w -> p (b w)")[:, 0:nk]
                                nc.scalar.activation(rl[:nq, h, 0:nk], src, ACT.Relu, scale=D ** -0.5).then_inc(ix_relu.sem, 1)
                        r = 0
                        for q in range(nt):
                            if q in dots_at and units:
                                relu(dots_at[q])
                            if q >= 2:
                                act.wait_ge(S["out"][q % 2].sem, S["out"][q % 2].at(l, 16 * (q // 2)))
                            for j in range(NJ):
                                act.wait_ge(S["mm"].sem, S["mm"].at(l, 3 * q + j + 1))
                                nc.scalar.activation(u[:, q % 2, cols(j)], PS[:, j, 0:JW], ACT.Copy).then_inc(S["ev"].sem, 1)
                                if r < 3 * len(rot) and (tiles.index(list(rot)[r // 3]), r % 3) < (q, j):
                                    swapped(r)
                                    r += 1
                        while r < 3 * len(rot):
                            swapped(r)
                            r += 1
                        for x in range(chunks * NU):
                            k, i = divmod(x, NU)
                            nq = UNITS[i][1]
                            if nt + x in dots_at:
                                relu(dots_at[nt + x])
                            if i == 0 and k:
                                act.wait_ge(S["tout"].sem, S["tout"].at(l, 32 * k))
                            act.wait_ge(S["tmm"].sem, S["tmm"].at(l, x + 1))
                            nc.scalar.activation(tout[:nq, i, :], PS[:nq, x % 3, 0:CW], ACT.Copy).then_inc(S["tev"].sem, 1)
                        if g == "lead":
                            act.wait_ge(iw_mm, l + 1)
                            nc.scalar.activation(iw[:, 0:NT, :], PS[:, 7, 0:NT * HI].rearrange("p (i h) -> p i h", h=HI), ACT.Copy,
                                                 scale=HI ** -0.5)
                            nc.scalar.activation(iw[:TS, NT, :], PS[:TS, 7, NT * HI:NU * HI], ACT.Copy, scale=HI ** -0.5)

                    @block.gpsimd
                    def _(pool):
                        pool.wait_ge(S["rope"], l * 32 + 32)
                        for n, i in rot.items():
                            q = tiles.index(n)
                            t, rows = ROTATED[n]
                            pool.wait_ge(S["ev"].sem, S["ev"].at(l, 3 * q + 3))
                            nc.gpsimd.tensor_tensor(cosb[:rows, :], u[:rows, q % 2, :], tab[:rows, t, :], ALU.mult)\
                                .then_inc(S["prod"].sem, 1)
                            pool.wait_ge(S["swapped"].sem, S["swapped"].at(l, 3 * i + 3))
                            nc.gpsimd.tensor_tensor(us[:rows, q % 2, :], us[:rows, q % 2, :], tab[:rows, t + 1, :], ALU.mult)\
                                .then_inc(S["prod"].sem, 1)
                            pool.wait_ge(S["prod"].sem, S["prod"].at(l, 2 * i + 2))
                            if rows < P:
                                hold(pool)
                                nc.gpsimd.tensor_copy(us[rows:, q % 2, :], u[rows:, q % 2, :])
                            nc.gpsimd.tensor_tensor(us[:rows, q % 2, :], us[:rows, q % 2, :], cosb[:rows, :], ALU.add)\
                                .then_inc(S["sum"].sem, 1)
                            pool.wait_ge(S["sum"].sem, S["sum"].at(l, i + 1))
                        hold(pool)

                    @block.vector
                    def _(dve):
                        if not units:
                            return
                        total = 2 * sum(rounds)
                        isteps = 2 + 2 * len(units) - 1
                        step = Chain(dve, ix_step, l * isteps)
                        for i in range(2):
                            step(nc.vector.memset(bias[:, BOFF[i]:BOFF[i + 1]], 0.0))
                            nc.vector.memset(bias[0:64, BOFF[i + 1] - 64:BOFF[i + 1]], 8 * NEG)
                        done = 0
                        for y, i in enumerate(units):
                            q0, nq, nk = UNITS[i]
                            wk = work[:nq, 0:nk]
                            for h in range(HI):
                                dve.wait_ge(ix_relu.sem, ix_relu.at(l, HI * y + h + 1))
                                if h == 0:
                                    nc.vector.tensor_scalar(wk, rl[:nq, 0, 0:nk], iw[:nq, i, 0:1], None, ALU.mult)\
                                        .then_inc(ix_acc.sem, 1)
                                else:
                                    dve.wait_ge(ix_acc.sem, ix_acc.at(l, HI * y + h))
                                    nc.vector.scalar_tensor_tensor(wk, rl[:nq, h, 0:nk], iw[:nq, i, h:h + 1], wk,
                                                                   ALU.mult, ALU.add).then_inc(ix_acc.sem, 1)
                            dve.wait_ge(ix_acc.sem, ix_acc.at(l, HI * (y + 1)))
                            if i < NT:
                                step(nc.vector.memset(work[0:64, nk - 64:nk], NEG))

                            def pick(base):
                                nc.vector.max(top[:nq, :], wk).then_inc(ix_pick, 1)
                                dve.wait_ge(ix_pick, base + 1)
                                hold(dve)
                                nc.vector.match_replace(wk, top[:nq, :], wk, SENTINEL).then_inc(ix_pick, 1)
                                dve.wait_ge(ix_pick, base + 2)
                                hold(dve)
                            z0 = rounds[y]
                            hold(dve)
                            with dve.Fori(0, z0 // 4) as it:
                                for z in range(4):
                                    pick(it * 8 + l * total + (done + 2 * z))
                            for z in range(z0 // 4 * 4, z0):
                                pick(l * total + done + 2 * z)
                            done += 2 * z0
                            step(nc.vector.tensor_scalar(bias[:nq, BOFF[i]:BOFF[i] + nk], wk, SENTINEL, 8 * NEG,
                                                         ALU.not_equal, ALU.mult))
                        assert step.n == isteps
                        hold(dve)

        def attention(l, g, heads, maps, cat, col0, bias=None):
            S = att[g]
            hw = D // maps
            scale = hw ** -0.5
            rq, rk, cv = (R_AQ, R_AK, C_AV) if g == "a" else (R_BQ, R_BK, C_BV)
            prev = {0: 0, 1: -1}
            done_before = [prev.get(i, i - 1) for i in range(NU)]
            wb = 2 if g == "a" else 3
            last_in_slot = [i - wb if i >= wb else max(z for z in range(NU) if z % wb == i) - NU for i in range(NU)]
            gdone = [GEND[z] if z >= 0 else GEND[z + NU] - NG for z in last_in_slot]
            steps = 2 * NT + 2 * NU + 3 * NU if g == "a" else NU
            with ExitStack() as c:
                q = sb(c, f"{g}q", [D, 2, T])
                kb = sb(c, f"{g}k", [D, 2, T + PAST])
                v = sb(c, f"{g}v", [P, 2, NT + 5, D])
                pm = sb(c, f"{g}p", [P, wb, maps, TP])
                cb = sb(c, f"{g}c", [P, 2, TP]) if g == "a" else pm[:, :, 0, :]
                pt = sb(c, f"{g}pt", [P, 2, NT, P])
                mx = sb(c, f"{g}mx", [P, NU, maps])
                ngm = sb(c, f"{g}ngm", [P, NU, maps])
                sums = sb(c, f"{g}sums", [P, NU, maps])
                rs = sb(c, f"{g}rs", [P, NU, maps])

                def bank(i, m):
                    return 2 * (m if maps == 2 else i % 2)

                def scores_of(i, m):
                    b = bank(i, m)
                    return PS[:UNITS[i][1], b:b + 2, :].rearrange("p b w -> p (b w)")[:, 0:UNITS[i][2]]

                with nc.Block() as block:
                    @block.sync
                    def _(sp):
                        def load(h, s, k):
                            n = l * heads + h
                            sp.wait_ge(S["pv"].sem, S["pv"].at(n - 2))
                            pt_ = projT[bass.ds(l, 1)]
                            pn = projN[bass.ds(l, 1), :, bass.ds(h * D + cv, D)]
                            rows = lambda r: pt_[:, bass.ds(h * D + r, D), :].rearrange("a p t -> p (a t)")
                            for dst, src in (
                                    (q[:, s, :], rows(rq)),
                                    (kb[:, s, 0:TP], rows(rk)[:, 0:TP]),
                                    (kb[:, s, TP + PAST:], rows(rk)[:, TP:T]),
                                    (kb[:, s, TP:TP + PAST], io[g + "k"][bass.ds(l, 1), bass.ds(h, 1)].rearrange("a b p t -> p (a b t)")),
                                    (v[:, s, 0:NT, :], pn[:, 0:TP, :].rearrange("a (i p) c -> p (a i) c", p=P)),
                                    (v[:, s, NT:NT + 4, :], io[g + "v"][bass.ds(l, 1), bass.ds(h, 1)].rearrange("a b p i c -> p (a b i) c")),
                                    (v[:TS, s, NT + 4, :], pn[:, TP:T, :].rearrange("a p c -> p (a c)"))):
                                sp.dma_start(dst, src).then_inc(S["inn"][s].sem, 16)
                        in_pairs(sp, 0, heads, load)

                    @block.tensor
                    def _(pe):
                        def head(h, s, k):
                            n = l * heads + h
                            pe.wait_ge(S["inn"][s].sem, S["inn"][s].at(l * ((heads + 1 - s) // 2) + k))

                            def score(i):
                                q0, nq, nk = UNITS[i]
                                for m in range(maps):
                                    if maps == 2:
                                        pe.wait_ge(S["exp"].sem, S["exp"].at(n, 2 * i + m - 1))
                                    else:
                                        pe.wait_ge(S["negmax"].sem, S["negmax"].at(n, done_before[i]))
                                    hold(pe)
                                    r = slice(hw * m, hw * (m + 1))
                                    for a in range(0, nk, 512):
                                        b = min(nk, a + 512)
                                        mm = nc.tensor.matmul(PS[:nq, bank(i, m) + a // 512, 0:b - a], q[r, s, q0:q0 + nq],
                                                              kb[r, s, KEY0[i] + a:KEY0[i] + b], start=True, stop=True)
                                    mm.then_inc(S["scores"].sem, 1)

                            def turn(i):
                                q0, nq, nk = UNITS[i]
                                pe.wait_ge(S["comb" if g == "a" else "exp"].sem, S["comb" if g == "a" else "exp"].at(n, i + 1))
                                g0 = GEND[i] - len(GROUPS[i])
                                for z, grp in enumerate(GROUPS[i]):
                                    pe.wait_ge(S["ptc"].sem, S["ptc"].at(n, g0 + z - 1))
                                    hold(pe)
                                    for kt in grp:
                                        kw = min(P, nk - kt * P)
                                        mm = nc.tensor.transpose(PS[:kw, 4 + (g0 + z) % 2, (kt % 4) * P:(kt % 4) * P + nq],
                                                                 cb[:nq, i % wb, kt * P:kt * P + kw], ident[:nq, :nq])
                                    mm.then_inc(S["tr"].sem, 1)
                                pe.wait_ge(S["ptc"].sem, S["ptc"].at(n, GEND[i]))
                                pe.wait_ge(S["out"].sem, S["out"].at(n, done_before[i]))
                                hold(pe)
                                last = -(-nk // P) - 1
                                dst = PS[:nq, 6 + i % 2, 0:D]
                                for kt in range(last + 1):
                                    kw = min(P, nk - kt * P)
                                    mm = nc.tensor.matmul(dst, pt[:kw, i % 2, kt, 0:nq], v[:kw, s, VT0[i] + kt, :],
                                                          start=(kt == 0), stop=(kt == last))
                                mm.then_inc(S["pv"].sem, 1)
                            for i in range(NU + 2):
                                if i < NU:
                                    score(i)
                                if i >= 2:
                                    turn(i - 2)
                        in_pairs(pe, 0, heads, head)

                    @block.scalar
                    def _(act):
                        def head(h, s, k):
                            n = l * heads + h

                            def expo(i):
                                q0, nq, nk = UNITS[i]
                                for m in range(maps):
                                    act.wait_ge(S["negmax"].sem, S["negmax"].at(n, maps * i + m + 1))
                                    if maps == 2:
                                        act.wait_ge(S["comb"].sem, S["comb"].at(n, done_before[i]))
                                    else:
                                        act.wait_ge(S["inv"].sem, S["inv"].at(n - 1, i + 1))
                                    src = scores_of(i, m) if maps == 2 else pm[:nq, i % wb, 0, 0:nk]
                                    nc.scalar.activation(pm[:nq, i % wb, m, 0:nk], src, ACT.Exp, bias=ngm[:nq, i, m:m + 1],
                                                         scale=scale if maps == 2 else 1.0,
                                                         accum_out=sums[:nq, i, m:m + 1]).then_inc(S["exp"].sem, 1)

                            def copies(i):
                                q0, nq, nk = UNITS[i]
                                g0 = GEND[i] - len(GROUPS[i])
                                act.wait_ge(S["pv"].sem, S["pv"].at(n, done_before[i]))
                                for z, grp in enumerate(GROUPS[i]):
                                    act.wait_ge(S["tr"].sem, S["tr"].at(n, g0 + z + 1))
                                    kw = min(P, nk - grp[0] * P)
                                    src = PS[:kw, 4 + (g0 + z) % 2, 0:len(grp) * P].rearrange("p (t w) -> p t w", w=P)
                                    nc.scalar.activation(pt[:kw, i % 2, grp[0]:grp[-1] + 1, 0:nq], src[:, :, 0:nq], ACT.Copy)\
                                        .then_inc(S["ptc"].sem, 1)

                            def output(i):
                                q0, nq, nk = UNITS[i]
                                act.wait_ge(S["pv"].sem, S["pv"].at(n, i + 1))
                                o = PS[:nq, 6 + i % 2, 0:D]
                                by = 1.0
                                if g == "b":
                                    act.wait_ge(S["inv"].sem, S["inv"].at(n, i + 1))
                                    by = rs[:nq, i, 0:1]
                                nc.scalar.activation(cat[:nq, i, bass.ds(h * D + col0, D)], o, ACT.Copy, scale=by)\
                                    .then_inc(S["out"].sem, 1)
                            for i in range(NU + 3):
                                if i < NU:
                                    expo(i)
                                if 2 <= i < NU + 2:
                                    copies(i - 2)
                                if i >= 3:
                                    output(i - 3)
                        in_pairs(act, 0, heads, head)

                    @block.vector
                    def _(dve):
                        def head(h, s, k):
                            n = l * heads + h
                            step = Chain(dve, S["step"], n * steps)

                            def maxima(i):
                                q0, nq, nk = UNITS[i]
                                for m in range(maps):
                                    dve.wait_ge(S["scores"].sem, S["scores"].at(n, maps * i + m + 1))
                                    if g == "a":
                                        sc = scores_of(i, m)
                                        if i < NT:
                                            b = bank(i, m) * 512 + nk - 64
                                            step(nc.vector.memset(PS[0:64, b // 512, b % 512:b % 512 + 64], NEG))
                                        step(nc.vector.tensor_reduce(mx[:nq, i, m:m + 1], sc, AX, ALU.max))
                                        nc.vector.tensor_scalar(ngm[:nq, i, m:m + 1], mx[:nq, i, m:m + 1], -scale, None, ALU.mult)\
                                            .then_inc(S["negmax"].sem, 1)
                                    else:
                                        dve.wait_ge(S["tr"].sem, S["tr"].at(n, gdone[i]))
                                        hold(dve)
                                        step(nc.vector.tensor_tensor_reduce(
                                            out=pm[:nq, i % wb, 0, 0:nk], in0=scores_of(i, 0), in1=bias[:nq, BOFF[i]:BOFF[i] + nk],
                                            scale=scale, scalar=-3.4e38, op0=ALU.add, op1=ALU.max, accum_out=mx[:nq, i, 0:1]))
                                        nc.vector.tensor_scalar(ngm[:nq, i, 0:1], mx[:nq, i, 0:1], -1.0, None, ALU.mult)\
                                            .then_inc(S["negmax"].sem, 1)

                            def combine(i):
                                q0, nq, nk = UNITS[i]
                                dve.wait_ge(S["exp"].sem, S["exp"].at(n, 2 * i + 2))
                                step(nc.vector.reciprocal(rs[:nq, i, :], sums[:nq, i, :]))
                                step(nc.vector.tensor_tensor(rs[:nq, i, 1:2], rs[:nq, i, 1:2], neglam[:nq, :], ALU.mult))
                                step(nc.vector.tensor_scalar(pm[:nq, i % wb, 1, 0:nk], pm[:nq, i % wb, 1, 0:nk], rs[:nq, i, 1:2],
                                                             None, ALU.mult))
                                dve.wait_ge(S["tr"].sem, S["tr"].at(n, gdone[i]))
                                nc.vector.scalar_tensor_tensor(cb[:nq, i % wb, 0:nk], pm[:nq, i % wb, 0, 0:nk], rs[:nq, i, 0:1],
                                                               pm[:nq, i % wb, 1, 0:nk], ALU.mult, ALU.add)\
                                    .then_inc(S["comb"].sem, 1)

                            def invert(i):
                                q0, nq, nk = UNITS[i]
                                dve.wait_ge(S["exp"].sem, S["exp"].at(n, i + 1))
                                dve.wait_ge(S["out"].sem, S["out"].at(n - 1, i + 1))
                                nc.vector.reciprocal(rs[:nq, i, :], sums[:nq, i, :]).then_inc(S["inv"].sem, 1)
                            finish = combine if g == "a" else invert
                            maxima(0)
                            for i in range(1, NU):
                                maxima(i)
                                finish(i - 1)
                            finish(NU - 1)
                            assert step.n == steps
                        in_pairs(dve, 0, heads, head)

        def hgrn(l, cat, col0, space):
            with ExitStack() as c:
                zq = sb(c, "zq", [D, 2, T])
                zf = sb(c, "zf", [D, 2, T])
                v = sb(c, "cv", [P, 2, NU, D])
                s0 = sb(c, "s0", [D, 2, D])
                sout = sb(c, "sout", [D, 2, 2, D])
                eq, ef, qe, kd = (space[:D, z * T:(z + 1) * T] for z in range(4))
                sg = sb(c, "sg", [D, T])
                x2 = sb(c, "x2", [D, T])
                kk_ = sb(c, "ck", [D, T])
                b = sb(c, "cb", [D, T])
                e = sb(c, "ce", [D, 2, T])
                qL = sb(c, "qL", [D, 7, T])
                kL = sb(c, "kL", [D, 7, T])
                ebl = sb(c, "ebl", [D, NU])
                lc = sb(c, "lc", [D, 2, HC])
                lh = sb(c, "lh", [D, 2])
                st = sb(c, "st", [D, 2, D])
                kdT = sb(c, "kdT", [P, 2, D])
                md = sb(c, "md", [P, NL, 32])
                ad = sb(c, "ad", [P, 32])
                at_ = sb(c, "at", [P, 2, P])
                DSTEPS = 9 + NU + NT
                qi = {0: 1, 2: 2, 3: 3, 4: 4, 5: 5, 6: 6, 7: 7, 8: 8}
                ki = {1: 1, 2: 2, 3: 3, 4: 4, 5: 5, 6: 6, 7: 7, 9: 8}

                def span(item):
                    return TP if item in (2, 3) else T

                with nc.Block() as block:
                    @block.sync
                    def _(sp):
                        def load(h, s, k):
                            n = l * HC + h
                            sp.wait_ge(c_o.sem, c_o.at(n - 2))
                            sp.wait_ge(c_s.sem, c_s.at(n - 2))
                            pt_ = projT[bass.ds(l, 1)]
                            pn = projN[bass.ds(l, 1), :, bass.ds(h * D + C_CI, D)]
                            rows = lambda r: pt_[:, bass.ds(h * D + r, D), :].rearrange("a p t -> p (a t)")
                            for dst, src in (
                                    (zq[:, s, :], rows(R_CQ)), (zf[:, s, :], rows(R_CF)),
                                    (v[:, s, 0:NT, :], pn[:, 0:TP, :].rearrange("a (i p) c -> p (a i) c", p=P)),
                                    (v[:TS, s, NT, :], pn[:, TP:T, :].rearrange("a p c -> p (a c)")),
                                    (s0[:, s, :], io["s0"][bass.ds(l, 1), bass.ds(h, 1)].rearrange("a b p c -> p (a b c)"))):
                                sp.dma_start(dst, src).then_inc(c_in[s].sem, 16)
                        in_pairs(sp, 0, HC, load)

                    @block.scalar
                    def _(act):
                        def head(h, s, k):
                            n = l * HC + h
                            act.wait_ge(c_in[s].sem, c_in[s].at(l * ((HC + 1 - s) // 2) + k))
                            act.wait_ge(c_q.sem, c_q.at(n - 1))
                            nc.scalar.activation(eq, zq[:, s, :], ACT.Exp, scale=-1.0).then_inc(c_gate.sem, 1)
                            act.wait_ge(c_km.sem, c_km.at(n - 1))
                            nc.scalar.activation(ef, zf[:, s, :], ACT.Exp, scale=-1.0).then_inc(c_gate.sem, 1)
                            act.wait_ge(c_x.sem, c_x.at(n))
                            nc.scalar.activation(sg[:], sg[:], ACT.Ln)
                            nc.scalar.activation(x2[:], x2[:], ACT.Ln).then_inc(c_ln.sem, 1)
                            act.wait_ge(c_d.sem, c_d.at(n, 1))
                            act.wait_ge(c_s.sem, c_s.at(n - 1))
                            nc.scalar.activation(ebl[:, 0:NT], b[:, 0:TP].rearrange("p (i w) -> p i w", w=P)[:, :, P - 1], ACT.Exp)
                            nc.scalar.activation(ebl[:, NT:NU], b[:, T - 1:T], ACT.Exp).then_inc(c_last.sem, 1)
                            for item in range(10):
                                w = span(item)
                                act.wait_ge(c_d.sem, c_d.at(n, item + 1))
                                buf = e[:, item % 2, 0:w]
                                if item == 0:
                                    act.wait_ge(c_km.sem, c_km.at(n - 1))
                                    nc.scalar.activation(buf, b[:], ACT.Exp).then_inc(c_e.sem, 1)
                                elif item in (1, 8, 9):
                                    nc.scalar.activation(buf, buf, ACT.Exp).then_inc(c_e.sem, 1)
                                else:
                                    nc.scalar.activation(buf, buf, ACT.Abs).then_inc(c_abs, 1)
                                    act.wait_ge(c_abs, n * 6 + (item - 1))
                                    nc.scalar.activation(buf, buf, ACT.Exp, scale=-1.0).then_inc(c_e.sem, 1)
                            for t in range(NU):
                                act.wait_ge(c_att.sem, c_att.at(n, t + 1))
                                act.wait_ge(c_su.sem, c_su.at(n, {0: 0, 1: -1}.get(t, t - 1)))
                                act.wait_ge(c_attd.sem, c_attd.at(n, t + 1))
                                w = UNITS[t][1]
                                src = PS[:, t % 2, :]
                                if t < NT:
                                    nc.scalar.activation(at_[0:64, t % 2, 64:128], src[0:64, 0:64], ACT.Copy)
                                    nc.scalar.activation(at_[0:32, t % 2, 32:64], src[0:32, 64:96], ACT.Copy)
                                    nc.scalar.activation(at_[64:96, t % 2, 96:128], src[64:96, 64:96], ACT.Copy)
                                nc.scalar.activation(kdT[:w, t % 2, :], PS[:w, 2 + t % 2, 0:D], ACT.Copy).then_inc(c_attc.sem, 1)
                            act.wait_ge(c_s.sem, c_s.at(n))
                            act.dma_start(io["stateC"][bass.ds(l, 1), bass.ds(h, 1)].rearrange("a b p m c -> p (a b m) c"),
                                          sout[:, s, :, :]).then_inc(c_out[s].sem, 16)
                        in_pairs(act, 0, HC, head)
                        for s in range(2):
                            act.wait_ge(c_out[s].sem, c_out[s].at(l * ((HC + 1 - s) // 2) + (HC + 1 - s) // 2 - 1))
                        hold(act)

                    @block.gpsimd
                    def _(pool):
                        def head(h, s, k):
                            n = l * HC + h
                            pool.wait_ge(c_inv.sem, c_inv.at(n))
                            nc.gpsimd.tensor_tensor(eq, zq[:, s, :], eq, ALU.mult).then_inc(c_q.sem, 1)
                            pool.wait_ge(c_q.sem, c_q.at(n))
                            pool.wait_ge(c_att.sem, c_att.at(n - 1))
                            pool.wait_ge(c_o.sem, c_o.at(n - 1))
                            for item in range(10):
                                if item not in qi:
                                    continue
                                w = span(item)
                                pool.wait_ge(c_e.sem, c_e.at(n, item + 1))
                                dst = qe if item == 0 else qL[:, item - 2, 0:w]
                                nc.gpsimd.tensor_tensor(dst, eq[:, 0:w], e[:, item % 2, 0:w], ALU.mult).then_inc(c_qm.sem, 1)
                        in_pairs(pool, 0, HC, head)

                    @block.vector
                    def _(dve):
                        step = Chain(dve, c_dstep, l * (1 + HC * DSTEPS))
                        nc.vector.tensor_copy(lc[:, 0, :], lbf[:, bass.ds(l, 1), :].rearrange("p a h -> p (a h)"))
                        step(nc.vector.tensor_copy(lc[:, 1, :], omlb[:, bass.ds(l, 1), :].rearrange("p a h -> p (a h)")))

                        def head(h, s, k):
                            n = l * HC + h
                            step = Chain(dve, c_dstep, l * (1 + HC * DSTEPS) + (h * DSTEPS + 1))
                            step(nc.vector.tensor_copy(lh[:], lc[:, :, bass.ds(h, 1)].rearrange("p a h -> p (a h)")))
                            dve.wait_ge(c_gate.sem, c_gate.at(n, 1))
                            step(nc.vector.tensor_scalar(eq, eq, 3e38, 1.0, ALU.min, ALU.add))
                            nc.vector.reciprocal(eq, eq).then_inc(c_inv.sem, 1)
                            dve.wait_ge(c_gate.sem, c_gate.at(n, 2))
                            step(nc.vector.tensor_scalar(ef, ef, 1e30, None, ALU.min))
                            step(nc.vector.tensor_scalar(sg[:], ef, 1.0, None, ALU.add))
                            step(nc.vector.reciprocal(sg[:], sg[:]))
                            step(nc.vector.scalar_tensor_tensor(kk_[:], ef, lh[:, 1:2], sg[:], ALU.mult, ALU.mult))
                            step(nc.vector.tensor_scalar(sg[:], sg[:], lh[:, 1:2], lh[:, 0:1], ALU.mult, ALU.add))
                            step(nc.vector.tensor_scalar(x2[:], sg[:], 2.0 ** 60, 1.0, ALU.mult, ALU.min))
                            nc.vector.tensor_scalar(sg[:], sg[:], 2.0 ** -60, None, ALU.max).then_inc(c_x.sem, 1)
                            dve.wait_ge(c_ln.sem, c_ln.at(n))
                            for t in range(NU):
                                q0, w, _ = UNITS[t]
                                r = slice(q0, q0 + w)
                                ins = nc.vector.tensor_tensor_scan(b[:, r], sg[:, r], x2[:, r], 0.0, ALU.add, ALU.add)
                            ins.then_inc(c_d.sem, 1)
                            dve.wait_ge(c_d.sem, c_d.at(n, 1))
                            dve.wait_ge(c_attc.sem, c_attc.at(n - 1))

                            def diff(item):
                                if item >= 2:
                                    dve.wait_ge(c_qm.sem, c_qm.at(n, qi.get(item - 2, 1 if item == 3 else 8)))
                                    if item - 2 in ki:
                                        dve.wait_ge(c_km.sem, c_km.at(n, ki[item - 2]))
                                w = span(item)
                                if item == 1:
                                    bt = b[:, 0:TP].rearrange("p (i w) -> p i w", w=P)
                                    nc.vector.tensor_tensor(e[:, 1, 0:TP].rearrange("p (i w) -> p i w", w=P),
                                                            bt[:, :, P - 1:P].to_broadcast([D, NT, P]), bt, ALU.subtract)
                                    nc.vector.tensor_tensor(e[:, 1, TP:T], b[:, T - 1:T].to_broadcast([D, TS]), b[:, TP:T],
                                                            ALU.subtract).then_inc(c_d.sem, 1)
                                    return
                                hw, r = (HALVES[item - 2], HALVES[item - 2] - 1) if item < 8 else (1, 0)
                                bt = b[:, 0:w].rearrange("p (i w) -> p i w", w=2 * hw)
                                ref = bt[:, :, r:r + 1].to_broadcast([D, w // (2 * hw), 2 * hw])
                                ins = (ref, bt) if item == 9 else (bt, ref)
                                nc.vector.tensor_tensor(e[:, item % 2, 0:w].rearrange("p (i w) -> p i w", w=2 * hw),
                                                        ins[0], ins[1], ALU.subtract).then_inc(c_d.sem, 1)

                            def kmul(item):
                                if item not in ki:
                                    return
                                w = span(item)
                                dve.wait_ge(c_e.sem, c_e.at(n, item + 1))
                                dst = kd if item == 1 else kL[:, min(item, 8) - 2, 0:w]
                                nc.vector.tensor_tensor(dst, kk_[:, 0:w], e[:, item % 2, 0:w], ALU.mult).then_inc(c_km.sem, 1)
                            diff(1)
                            for item in range(2, 10):
                                diff(item)
                                kmul(item - 1)
                            kmul(9)
                            step(nc.vector.memset(st[:, 0, :], 0.0))
                            dve.wait_ge(c_last.sem, c_last.at(n))
                            dve.wait_ge(c_out[s].sem, c_out[s].at(l * ((HC + 1 - s) // 2) + k - 1))
                            for t in range(NU):
                                w = UNITS[t][1]
                                dve.wait_ge(c_att.sem, c_att.at(n, t + 1))
                                dve.wait_ge(c_o.sem, c_o.at(n, {0: 0, 1: -1}.get(t, t - 1)))
                                pd = PS[:w, t % 2, 96:96 + NL * 32].rearrange("p (l w) -> p l w", w=32)
                                step(nc.vector.tensor_tensor(md[:w], pd, lmask[:w], ALU.mult))
                                red = at_[:w, t % 2, 0:32] if t == NT else ad[:]
                                ins = nc.vector.tensor_reduce(red, md[:w].rearrange("p l w -> p w l"), AX, ALU.add)
                                if t < NT:
                                    step(ins)
                                    ins = nc.vector.tensor_tensor(at_[:, t % 2, :].rearrange("p (j w) -> p j w", w=32),
                                                                  ad[:].unsqueeze(1).to_broadcast([P, 4, 32]), bmask[:], ALU.mult)
                                ins.then_inc(c_attd.sem, 1)
                                dve.wait_ge(c_su.sem, c_su.at(n, t + 1))
                                if t > 0:
                                    dve.wait_ge(c_s.sem, c_s.at(n, t))
                                src = st[:, t % 2, :] if t < NT else s0[:, s, :]
                                dst = st[:, (t + 1) % 2, :] if t < NT - 1 else sout[:, s, t - NT + 1, :]
                                nc.vector.scalar_tensor_tensor(dst, src, ebl[:, t:t + 1], PS[:D, 6 + t % 2, 0:D],
                                                               ALU.mult, ALU.add).then_inc(c_s.sem, 1)
                            dve.wait_ge(c_o.sem, c_o.at(n))
                            oc = cat[:, :, bass.ds(h * D + col0, D)]
                            nc.vector.tensor_copy(oc[:, 0:NT, :], PS[:, 4, :].rearrange("p (i d) -> p i d", d=D))
                            nc.vector.tensor_copy(oc[:TS, NT, :], PS[:TS, 5, 0:D]).then_inc(c_tail.sem, 1)
                            assert step.n == DSTEPS, step.n
                        in_pairs(dve, 0, HC, head)

                    @block.tensor
                    def _(pe):
                        def head(h, s, k):
                            n = l * HC + h
                            pe.wait_ge(c_in[s].sem, c_in[s].at(l * ((HC + 1 - s) // 2) + k))
                            pe.wait_ge(c_qm.sem, c_qm.at(n))
                            pe.wait_ge(c_km.sem, c_km.at(n))

                            def products(t):
                                q0, w, _ = UNITS[t]
                                pe.wait_ge(c_attc.sem, c_attc.at(n, {0: 0, 1: -1}.get(t, t - 1)))
                                hold(pe)
                                bank = PS[:, t % 2, :]
                                pair = lambda dst, lv, sc, tc, m: nc.tensor.matmul(
                                    dst, kL[:, lv, q0 + sc:q0 + sc + m], qL[:, lv, q0 + tc:q0 + tc + m], start=True, stop=True)
                                if t < NT:
                                    pair(bank[0:64, 0:64], 0, 0, 64, 64)
                                    pair(bank[0:32, 64:96], 1, 0, 32, 32)
                                    pair(bank[64:96, 64:96], 1, 64, 96, 32)
                                for j in range(w // 32):
                                    for z in range(NL):
                                        pair(bank[32 * j:32 * j + 32, 96 + 32 * z:128 + 32 * z], 2 + z, 32 * j, 32 * j, 32)
                                nc.tensor.transpose(PS[:w, 2 + t % 2, 0:D], kd[:, q0:q0 + w], ident[:D, :D]).then_inc(c_att.sem, 1)

                            def outputs(t):
                                q0, w, _ = UNITS[t]
                                pe.wait_ge(c_attd.sem, c_attd.at(n, t + 1))
                                pe.wait_ge(c_attc.sem, c_attc.at(n, t + 1))
                                if t == 0:
                                    pe.wait_ge(c_tail.sem, c_tail.at(n - 1))
                                pe.wait_ge(c_s.sem, c_s.at(n, {0: 0, 1: -1}.get(t, t - 1)))
                                hold(pe)
                                nc.tensor.matmul(PS[:D, 6 + t % 2, 0:D], kdT[:w, t % 2, :], v[:w, s, t, :], start=True, stop=True)\
                                    .then_inc(c_su.sem, 1)
                                if t > 0:
                                    pe.wait_ge(c_s.sem, c_s.at(n, t))
                                    hold(pe)
                                dst = PS[:, 4, t * D:(t + 1) * D] if t < NT else PS[:TS, 5, 0:D]
                                state = st[:, t % 2, :] if t < NT else s0[:, s, :]
                                nc.tensor.matmul(dst, qe[:, q0:q0 + w], state, start=True, stop=False)
                                nc.tensor.matmul(dst, at_[:w, t % 2, 0:w], v[:w, s, t, :], start=False, stop=True)\
                                    .then_inc(c_o.sem, 1)
                            products(0)
                            for t in range(1, NU):
                                products(t)
                                outputs(t - 1)
                            outputs(NU - 1)
                        in_pairs(pe, 0, HC, head)

        def merge(l, cat, catT):
            with ExitStack() as c:
                cg = sb(c, "cg", [P, NU, HC * D])
                sq = sb(c, "msq", [P, NU, HA * D])
                ss = sb(c, "mss", [P, 2, NU, HA])
                groups = ((0, HA, 0, P_AG), (1, HC, HA * D + HB * D, P_CG))
                with nc.Block() as block:
                    @block.sync
                    def _(sp):
                        pn = projN[bass.ds(l, 1), :, C_CG:C_CG + HC * D]
                        sp.dma_start(cg[:, 0:NT, :], pn[:, 0:TP, :].rearrange("a (i p) c -> p (a i) c", p=P)).then_inc(mg_in, 16)
                        sp.dma_start(cg[:TS, NT, :], pn[:, TP:T, :].rearrange("a p c -> p (a c)")).then_inc(mg_in, 16)
                        sp.wait_ge(mg_in, l * 32 + 32)
                        hold(sp)

                    @block.scalar
                    def _(act):
                        for g, nh, c0, pg in groups:
                            if g == 1:
                                act.wait_ge(mg_ss, l * 2 + 1)
                            nc.scalar.activation(sq[:, 0:NT, 0:nh * D], cat[:, 0:NT, c0:c0 + nh * D], ACT.Square)
                            nc.scalar.activation(sq[:TS, NT, 0:nh * D], cat[:TS, NT, c0:c0 + nh * D], ACT.Square).then_inc(mg_sq, 1)
                        act.wait_ge(mg_ss, l * 2 + 2)
                        for g, nh, c0, pg in groups:
                            nc.scalar.activation(ss[:, g, 0:NT, 0:nh], ss[:, g, 0:NT, 0:nh], ACT.Sqrt, bias=epst[:], scale=1.0 / D)
                            nc.scalar.activation(ss[:TS, g, NT, 0:nh], ss[:TS, g, NT, 0:nh], ACT.Sqrt, bias=epst[:TS], scale=1.0 / D)\
                                .then_inc(mg_root, 1)
                        act.wait_ge(mg_in, l * 32 + 32)
                        nc.scalar.activation(cg[:, 0:NT, :], cg[:, 0:NT, :], ACT.Silu)
                        nc.scalar.activation(cg[:TS, NT, :], cg[:TS, NT, :], ACT.Silu).then_inc(mg_silu, 1)
                        for i in range(NU):
                            w = UNITS[i][1]
                            for z in range(2):
                                g = 2 * i + z
                                act.wait_ge(mg_tr.sem, mg_tr.at(l, g + 1))
                                src = PS[:, g % 8, :].rearrange("p (k w) -> p k w", w=P)[:, :, 0:w]
                                nc.scalar.activation(catT[:, 4 * z:4 * z + 4, UNITS[i][0]:UNITS[i][0] + w], src, ACT.Copy)\
                                    .then_inc(mg_ev.sem, 1)

                    @block.vector
                    def _(dve):
                        msteps = 6 + 3 * NU
                        step = Chain(dve, mg_step, l * msteps)
                        for g, nh, c0, pg in groups:
                            dve.wait_ge(mg_sq, l * 2 + g + 1)
                            sqh = sq[:, :, 0:nh * D].rearrange("p i (h d) -> p i h d", d=D)
                            nc.vector.tensor_reduce(ss[:, g, 0:NT, 0:nh], sqh[:, 0:NT], AX, ALU.add)
                            nc.vector.tensor_reduce(ss[:TS, g, NT, 0:nh], sqh[:TS, NT], AX, ALU.add).then_inc(mg_ss, 1)
                        dve.wait_ge(mg_root, l * 2 + 2)
                        for g, nh, c0, pg in groups:
                            step(nc.vector.reciprocal(ss[:, g, 0:NT, 0:nh], ss[:, g, 0:NT, 0:nh]))
                            step(nc.vector.reciprocal(ss[:TS, g, NT, 0:nh], ss[:TS, g, NT, 0:nh]))
                            if g == 0:
                                step(nc.vector.tensor_scalar(ss[:, 0, 0:NT, :], ss[:, 0, 0:NT, :], par[:, P_LI + 1:P_LI + 2], None, ALU.mult))
                                step(nc.vector.tensor_scalar(ss[:TS, 0, NT, :], ss[:TS, 0, NT, :], par[:TS, P_LI + 1:P_LI + 2], None, ALU.mult))
                        dve.wait_ge(mg_silu, l + 1)
                        for g, nh, c0, pg in groups:
                            gain = par[:, pg:pg + D]
                            for i in range(NU):
                                w = UNITS[i][1]
                                o = cat[:w, i, c0:c0 + nh * D].rearrange("p (h d) -> p h d", d=D)
                                step(nc.vector.tensor_tensor(o, o, ss[:w, g, i, 0:nh].unsqueeze(2).to_broadcast([w, nh, D]), ALU.mult))
                                ins = nc.vector.tensor_tensor(o, o, gain[:w].unsqueeze(1).to_broadcast([w, nh, D]), ALU.mult)
                                if g == 1:
                                    step(ins)
                                    ins = nc.vector.tensor_tensor(cat[:w, i, c0:c0 + nh * D], cat[:w, i, c0:c0 + nh * D], cg[:w, i, :], ALU.mult)
                                ins.then_inc(mg_cat, 1)
                        assert step.n == msteps

                    @block.tensor
                    def _(pe):
                        for i in range(NU):
                            q0, w, _ = UNITS[i]
                            pe.wait_ge(mg_cat, l * 2 * NU + NU + i + 1)
                            for z in range(2):
                                g = 2 * i + z
                                if g >= 8:
                                    pe.wait_ge(mg_ev.sem, mg_ev.at(l, g - 7))
                                hold(pe)
                                for kk in range(4):
                                    tr = nc.tensor.transpose(PS[:, g % 8, kk * P:kk * P + w],
                                                             cat[:w, i, (4 * z + kk) * P:(4 * z + kk + 1) * P], ident[:w, :w])
                                tr.then_inc(mg_tr.sem, 1)

        def project_add(l, g, kt, src):
            S = sig_add[g]
            with ExitStack() as c:
                w = sb(c, g, [P, 2, kt, P])
                with nc.Block() as block:
                    @block.sync
                    def _(sp):
                        def load(n, s, k):
                            sp.wait_ge(S["mm"].sem, S["mm"].at(l * KD + n - 2))
                            sp.dma_start(w[:, s, :, :], io[g][bass.ds(l, 1), bass.ds(n, 1)]
                                         .rearrange("a b p (k c) -> p (a b k) c", c=P)).then_inc(S["inn"][s].sem, 16)
                        in_pairs(sp, 0, KD, load)

                    @block.tensor
                    def _(pe):
                        def tile(n, s, k):
                            N = l * KD + n
                            pe.wait_ge(S["inn"][s].sem, S["inn"][s].at(l * (KD // 2) + k))
                            for j in range(NJ):
                                pe.wait_ge(S["add"].sem, S["add"].at(N - 2, j + 1))
                                for kk in range(kt):
                                    mm = nc.tensor.matmul(PS[:, 3 * s + j, 0:JW], w[:, s, kk, :], src[:, kk, cols(j)],
                                                          start=(kk == 0), stop=(kk == kt - 1))
                                mm.then_inc(S["mm"].sem, 1)
                        in_pairs(pe, 0, KD, tile)

                    @block.vector
                    def _(dve):
                        def tile(n, s, k):
                            N = l * KD + n
                            for j in range(NJ):
                                dve.wait_ge(S["mm"].sem, S["mm"].at(N, j + 1))
                                x = xT[:, bass.ds(n, 1), cols(j)].rearrange("p a t -> p (a t)")
                                nc.vector.tensor_tensor(x, PS[:, 3 * s + j, 0:JW], x, ALU.add).then_inc(S["add"].sem, 1)
                        in_pairs(dve, 0, KD, tile)

        def ffn_up(l, xn, hT):
            AW = T + 4
            CVW = AW - 2
            with ExitStack() as c:
                w = sb(c, "uw", [P, 2, 2, KD, P])
                a = sb(c, "ua", [P, 2, AW])
                cv = sb(c, "ucv", [P, 2, CVW])
                cw = sb(c, "ucw", [P, 2, 4])
                tail = sb(c, "utail", [P, NF, 4])
                pieces = {0: [(0, 2, JW)], 1: [(JW, JW + 2, JW)],
                          2: [(2 * JW, 2 * JW + 2, TP - 2 * JW), (TP, TP + 4, TS)]}
                with nc.Block() as block:
                    @block.sync
                    def _(sp):
                        def load(n, s, k):
                            sp.wait_ge(up_g.sem, up_g.at(l * NF + n - 2))
                            sp.dma_start(w[:, s].rearrange("p g k c -> p (g k c)"), io["wu"][bass.ds(l, 1), bass.ds(n, 1)]
                                         .rearrange("a b p c -> p (a b c)")).then_inc(up_in[s].sem, 16)
                        in_pairs(sp, 0, NF, load)
                        sp.wait_ge(up_conv.sem, up_conv.at(l * NF + NF - 1))
                        sp.dma_start(io["tails"][bass.ds(l, 1)].rearrange("a p f c -> p (a f) c"), tail[:]).then_inc(up_tail, 16)
                        sp.wait_ge(up_tail, l * 16 + 16)
                        hold(sp)

                    @block.tensor
                    def _(pe):
                        def tile(n, s, k):
                            N = l * NF + n
                            pe.wait_ge(up_in[s].sem, up_in[s].at(l * (NF // 2) + k))
                            for gate, mmsig, freed in ((0, up_a, up_ev), (1, up_g, up_mul)):
                                for j in range(NJ):
                                    pe.wait_ge(freed.sem, freed.at(N - 1, j + 1))
                                    for kk in range(KD):
                                        mm = nc.tensor.matmul(PS[:, 3 * gate + j, 0:JW], w[:, s, gate, kk, :], xn[:, kk, cols(j)],
                                                              start=(kk == 0), stop=(kk == KD - 1))
                                    mm.then_inc(mmsig.sem, 1)
                        in_pairs(pe, 0, NF, tile)

                    @block.scalar
                    def _(act):
                        def tile(n, s, k):
                            N = l * NF + n
                            act.wait_ge(up_conv.sem, up_conv.at(N - 2))
                            for j in range(NJ):
                                act.wait_ge(up_a.sem, up_a.at(N, j + 1))
                                for t0, a0, wd in pieces[j]:
                                    ins = nc.scalar.activation(a[:, s, a0:a0 + wd], PS[:, j, t0 - j * JW:t0 - j * JW + wd], ACT.Copy)
                                ins.then_inc(up_ev.sem, 1)
                            act.wait_ge(up_conv.sem, up_conv.at(N))
                            nc.scalar.activation(cv[:, s, :], cv[:, s, :], ACT.Silu).then_inc(up_silu.sem, 1)
                        in_pairs(act, 0, NF, tile)

                    @block.vector
                    def _(dve):
                        for s in range(2):
                            z = nc.vector.memset(a[:, s, 0:2], 0.0)
                        z.then_inc(up_zero, 1)
                        dve.wait_ge(up_zero, l + 1)

                        def tile(n, s, k):
                            N = l * NF + n
                            step = Chain(dve, up_step, N * 3)
                            nc.vector.tensor_copy(cw[:, s, :], par[:, bass.ds(n * 4 + P_CONV, 4)])
                            step(nc.vector.tensor_copy(a[:, s, TP + 2:TP + 4], par[:, bass.ds(n * 2 + P_HIST, 2)]))
                            dve.wait_ge(up_ev.sem, up_ev.at(N))
                            nc.vector.tensor_copy(tail[:, bass.ds(n, 1), 0:2].rearrange("p a c -> p (a c)"), a[:, s, TP:TP + 2])
                            nc.vector.tensor_copy(tail[:, bass.ds(n, 1), 2:4].rearrange("p a c -> p (a c)"), a[:, s, AW - 2:AW])
                            step(nc.vector.tensor_scalar(cv[:, s, :], a[:, s, 2:AW], cw[:, s, 2:3], cw[:, s, 3:4], ALU.mult, ALU.add))
                            step(nc.vector.scalar_tensor_tensor(cv[:, s, :], a[:, s, 1:AW - 1], cw[:, s, 1:2], cv[:, s, :],
                                                                ALU.mult, ALU.add))
                            nc.vector.scalar_tensor_tensor(cv[:, s, :], a[:, s, 0:AW - 2], cw[:, s, 0:1], cv[:, s, :],
                                                           ALU.mult, ALU.add).then_inc(up_conv.sem, 1)
                            dve.wait_ge(up_silu.sem, up_silu.at(N))
                            for j in range(NJ):
                                dve.wait_ge(up_g.sem, up_g.at(N, j + 1))
                                for t0, a0, wd in pieces[j]:
                                    ins = nc.vector.tensor_tensor(hT[:, bass.ds(n, 1), t0:t0 + wd].rearrange("p a t -> p (a t)"),
                                                                  PS[:, 3 + j, t0 - j * JW:t0 - j * JW + wd],
                                                                  cv[:, s, a0 - 2:a0 - 2 + wd], ALU.mult)
                                ins.then_inc(up_mul.sem, 1)
                        in_pairs(dve, 0, NF, tile)

        with nc.Fori(0, L) as l:
            load_params(l)
            cb_ = ExitStack()
            bias = sb(cb_, "bias", [P, NBIAS])
            iw = sb(cb_, "iw", [P, NU, HI])
            with ExitStack() as c:
                xn = sb(c, "xn", [P, KD, T])
                rms_norm(l * 2, par[:, P_N1:P_N1 + KD], xn)
                project(l, "lead", xn, iw)
                project(l, "rest", xn, iw, bias)
            with ExitStack() as c:
                cat = sb(c, "cat", [P, NU, DM])
                attention(l, "b", HB, 1, cat, HA * D, bias)
                attention(l, "a", HA, 2, cat, 0)
                hgrn(l, cat, (HA + HB) * D, bias)
                catT = sb(c, "catT", [P, KD, T])
                merge(l, cat, catT)
                project_add(l, "wo", KD, catT)
            cb_.close()
            with ExitStack() as c:
                hT = sb(c, "hT", [P, NF, T])
                with ExitStack() as c2:
                    xn = sb(c2, "xn2", [P, KD, T])
                    rms_norm(l * 2 + 1, par[:, P_N2:P_N2 + KD], xn)
                    ffn_up(l, xn, hT)
                project_add(l, "wd", NF, hT)

        yT = sb(ctx, "yT", [P, KD, T])
        rms_norm(2 * L, fgain, yT)
        with nc.Block() as block:
            @block.sync
            def _(sp):
                sp.dma_start(io["yT"].rearrange("(k p) t -> p k t", p=P), yT[:]).then_inc(s_yout, 16)
                sp.wait_ge(s_yout, 16)


def kernel(**inputs):
    import math
    import numpy as np
    import concourse.bacc as bacc
    from concourse.bass_utils import run_bass_kernel_spmd

    a = {k: np.asarray(v) for k, v in inputs.items()}
    nc = bacc.Bacc("TRN2", target_bir_lowering=False, num_devices=1)

    names = ["aq", "ak", "av", "bq", "bk", "bv", "iq", "ik", "iw", "cq", "cf", "ci", "cg"]
    sizes = [384, 384, 384, 320, 320, 320, 256, 64, 4, 320, 320, 320, 320]
    off = np.concatenate([[0], np.cumsum(sizes)])
    col = {nm: np.arange(off[i], off[i + 1]) for i, nm in enumerate(names)}
    w_in = a["w_in"]
    take = lambda *which: w_in[:, :, np.concatenate([col[x] for x in which])]
    wf = take("iq", "ik", "bq", "bk", "cq", "cf")
    wf = np.concatenate([wf, np.zeros((L, DM, R_AQ - wf.shape[2]), np.float32), take("aq", "ak")], axis=2)
    wn = take("av", "bv", "ci", "cg")

    def tiles(w, width):
        l_, k_, n_ = w.shape
        return w.reshape(l_, k_ // P, P, n_ // width, width).transpose(0, 3, 2, 1, 4).reshape(l_, n_ // width, P, -1)

    up = tiles(a["ffn_up"], P)
    wu = np.stack([up[:, :NF], up[:, NF:]], axis=3)

    pos = np.concatenate([np.arange(TP), PAST + np.arange(TS)]).astype(np.float32)

    def table(width):
        inv = (10000.0 ** (-np.arange(0, width, 2, dtype=np.float32).astype(np.float64) / width)).astype(np.float32)
        ang = (pos[None, :] * inv[:, None]).astype(np.float32).astype(np.float64)
        cos = np.concatenate([np.cos(ang), np.cos(ang)])
        sin = np.concatenate([-np.sin(ang), np.sin(ang)])
        return [np.tile(x, (P // width, 1)).astype(np.float32) for x in (cos, sin)]

    def swap(width):
        p = np.arange(P)
        m = np.zeros((P, P), np.float32)
        m[p, p // width * width + (p % width + width // 2) % width] = 1
        return m

    s_, t_ = np.arange(32)[:, None], np.arange(32)[None, :]
    lm = [((s_ // (2 * h) == t_ // (2 * h)) & (s_ % (2 * h) < h) & (t_ % (2 * h) >= h)) for h in (16, 8, 4, 2)]
    lm.append((s_ // 2 == t_ // 2) & (s_ <= t_))
    lmask = np.tile(np.stack(lm, axis=1), (4, 1, 1)).astype(np.float32)
    bmask = np.repeat((np.arange(P)[:, None] // 32 == np.arange(4)[None, :])[:, :, None], 32, axis=2).astype(np.float32)

    def per_feature(x, k):
        return x.reshape(L, k, P).transpose(0, 2, 1)

    conv = np.concatenate([a["ffn_conv_w"], a["ffn_conv_b"][:, None]], axis=1)
    conv = conv.reshape(L, 4, NF, P).transpose(0, 3, 2, 1).reshape(L, P, NF * 4)
    hist = a["state_ffn_conv"][:, 0].reshape(L, 2, NF, P).transpose(0, 3, 2, 1).reshape(L, P, NF * 2)
    wide = lambda x: np.broadcast_to(x[:, None, :], (L, P, x.shape[1]))
    li = np.array([[0.8 - 0.6 * math.exp(-0.3 * i), 1.0 - (0.8 - 0.6 * math.exp(-0.3 * i))] for i in range(L)], np.float32)
    params = np.concatenate([
        per_feature(a["norm1"], KD), per_feature(a["norm2"], KD), conv, hist, wide(a["a_norm"]), wide(a["c_norm"]),
        wide(a["lam_q1"]), wide(a["lam_k1"]), wide(a["lam_q2"]), wide(a["lam_k2"]), wide(li)], axis=2)

    arrays = {
        "xT": np.concatenate([a["x_prompt"][0], a["x_sample"][0]]).T,
        "wf": tiles(wf, P), "wn": tiles(wn, CW), "wiw": take("iw").reshape(L, KD, P, HI).transpose(0, 2, 1, 3), "wo": tiles(a["w_out"], P), "wu": wu.reshape(L, NF, P, -1),
        "wd": tiles(a["ffn_down"], P), "rope": np.stack(table(32) + table(64)), "swapA": swap(32), "swapB": swap(64),
        "ident": np.eye(P, dtype=np.float32), "ones": np.ones((P, P), np.float32), "lmask": lmask, "bmask": bmask,
        "fgain": a["final_norm"].reshape(KD, P).T, "clow": a["c_lower"].reshape(L, HC, D).transpose(2, 0, 1),
        "params": params, "kidx": a["cache_b_kidx"][:, 0].transpose(0, 2, 1), "s0": a["state_c"][:, 0],
        "ak": a["cache_a_k"][:, 0].transpose(0, 2, 3, 1), "bk": a["cache_b_k"][:, 0].transpose(0, 2, 3, 1),
        "av": a["cache_a_v"][:, 0].reshape(L, PAST // P, P, HA, D).transpose(0, 3, 2, 1, 4),
        "bv": a["cache_b_v"][:, 0].reshape(L, PAST // P, P, HB, D).transpose(0, 3, 2, 1, 4),
    }
    outs = {"yT": (DM, T), "projT": (L, NPT * P, T), "projN": (L, T, WN), "stateC": (L, HC, D, 2, D), "tails": (L, P, NF, 4)}
    arrays = {"in_" + k: np.ascontiguousarray(v) for k, v in arrays.items()}
    io = {k[3:]: nc.dram_tensor(k, v.shape, F32, kind="ExternalInput").ap() for k, v in arrays.items()}
    io.update({k: nc.dram_tensor("out_" + k, v, F32, kind="ExternalOutput").ap() for k, v in outs.items()})
    build(nc, io)
    r = run_bass_kernel_spmd(nc, [arrays], core_ids=[0]).results[0]
    y, pT, pN, sC, tl = (np.asarray(r["out_" + k]) for k in outs)

    def group(t0, t1, m):
        rows = lambda r0, h: pT[:, r0:r0 + h * D, t0:t1].reshape(L, h, D, t1 - t0).transpose(0, 3, 1, 2)[:, None]
        vals = lambda c0, h: pN[:, t0:t1, c0:c0 + h * D].reshape(L, 1, t1 - t0, h, D)
        tail = tl[:, :, :, 2 * m:2 * m + 2].transpose(0, 3, 2, 1).reshape(L, 1, 2, DFF)
        return (rows(R_AK, HA), vals(C_AV, HA), rows(R_BK, HB), vals(C_BV, HB), rows(R_IK, 1)[:, :, :, 0],
                sC[:, None, :, :, m], tail)
    return (y[:, :TP].T[None], y[:, TP:].T[None]) + group(0, TP, 0) + group(TP, T, 1)
```
